# Optimizing a Trainium2 kernel written in Bass

```python
import math
import jax, jax.numpy as jnp
from jax import lax
import numpy as np
import jax
import jax.numpy as jnp

D_MODEL = 1024
BATCH = 1
SEQ = 512
DEPTH = 1

CHUNK = 64
D_MIX = 2 * D_MODEL
SSD_WIDTH = D_MIX // 2
SSD_HEAD_DIM = 64
SSD_HEADS = SSD_WIDTH // SSD_HEAD_DIM
SSD_GROUPS = 2
SSD_HPG = SSD_HEADS // SSD_GROUPS
SSD_STATE = 128
SSD_CONV = 4
SSD_CONV_CH = SSD_WIDTH + 2 * SSD_GROUPS * SSD_STATE
SC_WIDTH = D_MIX - SSD_WIDTH
SC_GROUP_DIM = 64
SC_GROUPS = SC_WIDTH // SC_GROUP_DIM
SC_CONV = 3
IN_COLS = SSD_WIDTH + SSD_CONV_CH + SSD_HEADS + 3 * SC_WIDTH
N_EXPERT_GROUPS = 4
EXPERTS_PER_GROUP = 8
N_EXPERTS = N_EXPERT_GROUPS * EXPERTS_PER_GROUP
TOP_K_IN_GROUP = 2
D_FF_EXPERT = D_MODEL // 2
EXPERT_BLOCK = 128
EPS = 1e-6


def rmsnorm(x, g):
    xf = x.astype(jnp.float32)
    y = xf * lax.rsqrt(jnp.mean(xf * xf, axis=-1, keepdims=True) + EPS)
    return (y * g.astype(jnp.float32)).astype(x.dtype)

def grouped_rmsnorm(x, g, n_groups):
    shp = x.shape
    xf = x.astype(jnp.float32).reshape(*shp[:-1], n_groups, shp[-1] // n_groups)
    y = xf * lax.rsqrt(jnp.mean(xf * xf, axis=-1, keepdims=True) + EPS)
    return (y.reshape(shp) * g.astype(jnp.float32)).astype(x.dtype)

def causal_depthwise_conv(x, w):
    k = w.shape[0]
    return lax.conv_general_dilated(
        x, w[:, None, :].astype(x.dtype), window_strides=(1,), padding=[(k - 1, 0)],
        dimension_numbers=("NWC", "WIO", "NWC"), feature_group_count=x.shape[-1])

def ssd_chunked_scan(x, dt, a, bmat, cmat):
    bsz, seqlen = x.shape[0], x.shape[1]
    nc = seqlen // CHUNK
    f32 = jnp.float32
    xdt = (x.astype(f32) * dt[..., None]).reshape(bsz, nc, CHUNK, SSD_GROUPS, SSD_HPG, SSD_HEAD_DIM)
    bc = bmat.astype(f32).reshape(bsz, nc, CHUNK, SSD_GROUPS, SSD_STATE)
    cc = cmat.astype(f32).reshape(bsz, nc, CHUNK, SSD_GROUPS, SSD_STATE)
    a_dt = (dt * a.astype(f32)).reshape(bsz, nc, CHUNK, SSD_GROUPS, SSD_HPG)
    ac = jnp.cumsum(a_dt, axis=2).transpose(0, 1, 3, 4, 2)
    seg = ac[..., :, None] - ac[..., None, :]
    causal = jnp.tril(jnp.ones((CHUNK, CHUNK), dtype=bool))
    decay_in = jnp.exp(jnp.where(causal, seg, -jnp.inf))
    cb = jnp.einsum("bclgn,bcsgn->bcgls", cc, bc)
    y_diag = jnp.einsum("bcgls,bcgrls,bcsgrp->bclgrp", cb, decay_in, xdt)
    decay_to_end = jnp.exp(ac[..., -1:] - ac)
    states = jnp.einsum("bclgn,bcgrl,bclgrp->bcgrpn", bc, decay_to_end, xdt)
    chunk_decay = jnp.exp(ac[..., -1])

    def step(carry, inp):
        st, dec = inp
        return carry * dec[..., None, None] + st, carry

    init = jnp.zeros((bsz, SSD_GROUPS, SSD_HPG, SSD_HEAD_DIM, SSD_STATE), f32)
    _, prev = lax.scan(step, init, (jnp.moveaxis(states, 1, 0), jnp.moveaxis(chunk_decay, 1, 0)))
    prev = jnp.moveaxis(prev, 0, 1)
    y_off = jnp.einsum("bclgn,bcgrpn,bcgrl->bclgrp", cc, prev, jnp.exp(ac))
    return (y_diag + y_off).reshape(bsz, seqlen, SSD_HEADS, SSD_HEAD_DIM)

def hybrid_mixer(hn, w_in, ssd_conv_w, ssd_conv_b, dt_bias, a_log, d_skip, ssd_norm,
                 sc_conv_w, sc_norm, w_out):
    bsz, seqlen, _ = hn.shape
    proj = hn @ w_in
    o1 = SSD_WIDTH
    o2 = o1 + SSD_CONV_CH
    o3 = o2 + SSD_HEADS
    o4 = o3 + SC_WIDTH
    o5 = o4 + SC_WIDTH
    z, xbc, dt_raw, sc_b, sc_c, sc_v = jnp.split(proj, [o1, o2, o3, o4, o5], axis=-1)
    xbc = jax.nn.silu(causal_depthwise_conv(xbc, ssd_conv_w) + ssd_conv_b)
    xs, bm, cm = jnp.split(xbc, [SSD_WIDTH, SSD_WIDTH + SSD_GROUPS * SSD_STATE], axis=-1)
    dt = jax.nn.softplus(dt_raw.astype(jnp.float32) + dt_bias.astype(jnp.float32))
    a = -jnp.exp(a_log.astype(jnp.float32))
    xh = xs.reshape(bsz, seqlen, SSD_HEADS, SSD_HEAD_DIM)
    y = ssd_chunked_scan(xh, dt, a,
                         bm.reshape(bsz, seqlen, SSD_GROUPS, SSD_STATE),
                         cm.reshape(bsz, seqlen, SSD_GROUPS, SSD_STATE))
    y = y + d_skip.astype(jnp.float32)[:, None] * xh.astype(jnp.float32)
    y = y.reshape(bsz, seqlen, SSD_WIDTH).astype(hn.dtype)
    ssd_out = grouped_rmsnorm(y * jax.nn.silu(z), ssd_norm, SSD_GROUPS)
    sc = sc_b * causal_depthwise_conv(sc_c * sc_v, sc_conv_w)
    sc_out = grouped_rmsnorm(sc, sc_norm, SC_GROUPS)
    return jnp.concatenate([ssd_out, sc_out], axis=-1) @ w_out

def hierarchical_moe(hn, w_router_group, w_router_expert, w_gate, w_up, w_down):
    bsz, seqlen, d = hn.shape
    tokens = hn.reshape(-1, d)
    n = tokens.shape[0]
    g_logits = (tokens @ w_router_group).astype(jnp.float32)
    g_probs = jax.nn.softmax(g_logits, axis=-1)
    g_idx = jnp.argmax(g_logits, axis=-1)
    g_w = jnp.take_along_axis(g_probs, g_idx[:, None], axis=1)
    e_logits = jnp.einsum("nd,gde->nge", tokens, w_router_expert).astype(jnp.float32)
    e_sel = jnp.take_along_axis(e_logits, g_idx[:, None, None], axis=1)[:, 0]
    top_v, top_i = lax.top_k(e_sel, TOP_K_IN_GROUP)
    gates = g_w * jax.nn.softmax(top_v, axis=-1)
    expert_id = (g_idx[:, None] * EXPERTS_PER_GROUP + top_i).reshape(-1).astype(jnp.int32)
    token_id = jnp.repeat(jnp.arange(n, dtype=jnp.int32), TOP_K_IN_GROUP)
    gate_flat = gates.reshape(-1)
    m = n * TOP_K_IN_GROUP
    order = jnp.argsort(expert_id)
    sorted_e = expert_id[order]
    counts = jnp.bincount(expert_id, length=N_EXPERTS)
    padded_counts = ((counts + EXPERT_BLOCK - 1) // EXPERT_BLOCK) * EXPERT_BLOCK
    padded_end = jnp.cumsum(padded_counts)
    padded_start = padded_end - padded_counts
    start = jnp.cumsum(counts) - counts
    rank = jnp.arange(m, dtype=jnp.int32) - start[sorted_e]
    dest = padded_start[sorted_e] + rank
    p_rows = ((m + N_EXPERTS * EXPERT_BLOCK + EXPERT_BLOCK - 1) // EXPERT_BLOCK) * EXPERT_BLOCK
    n_blocks = p_rows // EXPERT_BLOCK
    row_token = jnp.zeros((p_rows,), jnp.int32).at[dest].set(token_id[order])
    row_gate = jnp.zeros((p_rows,), jnp.float32).at[dest].set(gate_flat[order])
    block_expert = jnp.clip(
        jnp.searchsorted(padded_end, jnp.arange(n_blocks) * EXPERT_BLOCK, side="right"),
        0, N_EXPERTS - 1).astype(jnp.int32)
    xs = tokens[row_token].reshape(n_blocks, EXPERT_BLOCK, d)

    def run_block(args):
        xb, e = args
        return (jax.nn.silu(xb @ w_gate[e]) * (xb @ w_up[e])) @ w_down[e]

    ys = lax.map(run_block, (xs, block_expert)).reshape(p_rows, d)
    out = jnp.zeros((n, d), jnp.float32).at[row_token].add(ys.astype(jnp.float32) * row_gate[:, None])
    return out.reshape(bsz, seqlen, d).astype(hn.dtype)

def first_inputs(seed: int = 0) -> dict:
    key = jax.random.key(seed)
    ks = jax.random.split(key, 24)
    f32 = jnp.float32

    def nrm(k, shape, scale):
        return jax.random.normal(k, shape, f32) * scale

    x = nrm(ks[0], (BATCH, SEQ, D_MODEL), 1.0)
    norm_mix = 1.0 + nrm(ks[1], (DEPTH, D_MODEL), 0.02)
    w_in = nrm(ks[2], (DEPTH, D_MODEL, IN_COLS), D_MODEL ** -0.5)
    ssd_conv_w = nrm(ks[3], (DEPTH, SSD_CONV, SSD_CONV_CH), SSD_CONV ** -0.5)
    ssd_conv_b = nrm(ks[4], (DEPTH, SSD_CONV_CH), 0.01)
    dt0 = jnp.exp(jax.random.uniform(ks[5], (DEPTH, SSD_HEADS), f32,
                                     minval=math.log(1e-3), maxval=math.log(1e-1)))
    dt_bias = dt0 + jnp.log(-jnp.expm1(-dt0))
    a_log = jnp.log(jax.random.uniform(ks[6], (DEPTH, SSD_HEADS), f32, minval=1.0, maxval=16.0))
    d_skip = 1.0 + nrm(ks[7], (DEPTH, SSD_HEADS), 0.1)
    ssd_norm = 1.0 + nrm(ks[8], (DEPTH, SSD_WIDTH), 0.02)
    sc_conv_w = nrm(ks[9], (DEPTH, SC_CONV, SC_WIDTH), SC_CONV ** -0.5)
    sc_norm = 1.0 + nrm(ks[10], (DEPTH, SC_WIDTH), 0.02)
    w_out = nrm(ks[11], (DEPTH, D_MIX, D_MODEL), D_MIX ** -0.5)
    norm_ffn = 1.0 + nrm(ks[12], (DEPTH, D_MODEL), 0.02)
    w_router_group = nrm(ks[13], (DEPTH, D_MODEL, N_EXPERT_GROUPS), D_MODEL ** -0.5)
    w_router_expert = nrm(ks[14], (DEPTH, N_EXPERT_GROUPS, D_MODEL, EXPERTS_PER_GROUP), D_MODEL ** -0.5)
    w_gate = nrm(ks[15], (DEPTH, N_EXPERTS, D_MODEL, D_FF_EXPERT), D_MODEL ** -0.5)
    w_up = nrm(ks[16], (DEPTH, N_EXPERTS, D_MODEL, D_FF_EXPERT), D_MODEL ** -0.5)
    w_down = nrm(ks[17], (DEPTH, N_EXPERTS, D_FF_EXPERT, D_MODEL), D_FF_EXPERT ** -0.5)
    final_norm = 1.0 + nrm(ks[18], (D_MODEL,), 0.02)
    return {"x": x, "norm_mix": norm_mix, "w_in": w_in, "ssd_conv_w": ssd_conv_w,
            "ssd_conv_b": ssd_conv_b, "dt_bias": dt_bias, "a_log": a_log, "d_skip": d_skip,
            "ssd_norm": ssd_norm, "sc_conv_w": sc_conv_w, "sc_norm": sc_norm, "w_out": w_out,
            "norm_ffn": norm_ffn, "w_router_group": w_router_group,
            "w_router_expert": w_router_expert, "w_gate": w_gate, "w_up": w_up,
            "w_down": w_down, "final_norm": final_norm}

def first_block(x, norm_mix, w_in, ssd_conv_w, ssd_conv_b, dt_bias, a_log, d_skip, ssd_norm,
              sc_conv_w, sc_norm, w_out, norm_ffn, w_router_group, w_router_expert,
              w_gate, w_up, w_down, final_norm):
    h = x
    for i in range(DEPTH):
        hn = rmsnorm(h, norm_mix[i])
        h = h + hybrid_mixer(hn, w_in[i], ssd_conv_w[i], ssd_conv_b[i], dt_bias[i], a_log[i],
                             d_skip[i], ssd_norm[i], sc_conv_w[i], sc_norm[i], w_out[i])
        hn = rmsnorm(h, norm_ffn[i])
        h = h + hierarchical_moe(hn, w_router_group[i], w_router_expert[i],
                                 w_gate[i], w_up[i], w_down[i])
    return rmsnorm(h, final_norm)


GRID_W = 64
CTX_LEN = 256
ATT_HEADS = 16
ATT_KV_HEADS = 4
ATT_HEAD_DIM = 64
ATT_GROUP = ATT_HEADS // ATT_KV_HEADS
WINDOW = 128
ATT_BLOCK = 128
ROPE_BASE = 10000.0
ATT_SCALE = ATT_HEAD_DIM ** -0.5
ML_HEADS = 4
ML_QK_DIM = 128
ML_V_DIM = 256
ML_CHUNK = 128
D_FF = 2816
CONV_W = 3
NEG_INF = -1e30

ATT_Q_W = ATT_HEADS * ATT_HEAD_DIM
ATT_KV_W = ATT_KV_HEADS * ATT_HEAD_DIM
ML_QK_W = ML_HEADS * ML_QK_DIM
ML_V_W = ML_HEADS * ML_V_DIM
ML_GATE_W = 2 * 2 * ML_HEADS
IN_SPLITS = (ATT_Q_W, ATT_KV_W, ATT_KV_W, ML_QK_W, ML_QK_W, ML_V_W, ML_V_W, ML_GATE_W, D_MODEL, D_MODEL)
IN_W = ATT_Q_W + 2 * ATT_KV_W + 2 * ML_QK_W + 2 * ML_V_W + ML_GATE_W + 2 * D_MODEL


def rms_norm(x, w):
    xf = x.astype(jnp.float32)
    y = xf * lax.rsqrt(jnp.mean(xf * xf, axis=-1, keepdims=True) + EPS)
    return (y * w.astype(jnp.float32)).astype(x.dtype)

def modulate(h, shift, scale):
    return h * (1 + scale[:, None, :]) + shift[:, None, :]

def heads(a, n_heads, head_dim):
    return a.reshape(a.shape[0], a.shape[1], n_heads, head_dim)

def split_in_proj(p):
    parts, start = [], 0
    for width in IN_SPLITS:
        parts.append(p[..., start:start + width])
        start += width
    return parts

def axial_rope(rows):
    row = jnp.repeat(jnp.arange(rows, dtype=jnp.float32), GRID_W)
    col = jnp.tile(jnp.arange(GRID_W, dtype=jnp.float32), rows)
    n_freq = ATT_HEAD_DIM // 4
    inv_freq = ROPE_BASE ** (-jnp.arange(n_freq, dtype=jnp.float32) / n_freq)
    ang = jnp.concatenate([row[:, None] * inv_freq, col[:, None] * inv_freq], axis=-1)
    return jnp.cos(ang)[:, None, :], jnp.sin(ang)[:, None, :]

def apply_rope(x, cos, sin):
    xf = x.astype(jnp.float32)
    half = x.shape[-1] // 2
    x1, x2 = xf[..., :half], xf[..., half:]
    return jnp.concatenate([x1 * cos - x2 * sin, x1 * sin + x2 * cos], axis=-1).astype(x.dtype)

def windowed_gqa(q, k, v, k_ctx, v_ctx, sink):
    B, L, H, dh = q.shape
    T = ATT_BLOCK
    nb = L // T
    C = k_ctx.shape[1]
    qb = q.reshape(B, nb, T, ATT_KV_HEADS, ATT_GROUP, dh).swapaxes(0, 1)

    def band(a):
        ap = jnp.pad(a, ((0, 0), (T, T), (0, 0), (0, 0))).reshape(B, nb + 2, T, ATT_KV_HEADS, dh)
        w = jnp.concatenate([ap[:, :-2], ap[:, 1:-1], ap[:, 2:]], axis=2)
        return w.swapaxes(0, 1)

    kb, vb = band(k), band(v)
    sink_b = jnp.broadcast_to(sink.astype(jnp.float32).reshape(1, ATT_KV_HEADS, ATT_GROUP, 1, 1),
                              (B, ATT_KV_HEADS, ATT_GROUP, T, 1))
    key_off = jnp.arange(3 * T) - T
    rel = key_off[None, :] - jnp.arange(T)[:, None]

    def one_block(args):
        blk, qblk, kblk, vblk = args
        k_abs = blk * T + key_off
        valid = (jnp.abs(rel) <= WINDOW) & ((k_abs >= 0) & (k_abs < L))[None, :]
        s_lat = jnp.einsum('btkgd,bskd->bkgts', qblk, kblk).astype(jnp.float32) * ATT_SCALE
        s_lat = jnp.where(valid, s_lat, NEG_INF)
        s_ctx = jnp.einsum('btkgd,bskd->bkgts', qblk, k_ctx).astype(jnp.float32) * ATT_SCALE
        p = jax.nn.softmax(jnp.concatenate([s_lat, s_ctx, sink_b], axis=-1), axis=-1).astype(v.dtype)
        return (jnp.einsum('bkgts,bskd->btkgd', p[..., :3 * T], vblk)
                + jnp.einsum('bkgts,bskd->btkgd', p[..., 3 * T:3 * T + C], v_ctx))

    o = lax.map(one_block, (jnp.arange(nb), qb, kb, vb))
    return o.swapaxes(0, 1).reshape(B, L, H * dh)

def context_gqa(q_ctx, k_ctx, v_ctx, sink):
    B, C, H, dh = q_ctx.shape
    qg = q_ctx.reshape(B, C, ATT_KV_HEADS, ATT_GROUP, dh)
    s = jnp.einsum('btkgd,bskd->bkgts', qg, k_ctx).astype(jnp.float32) * ATT_SCALE
    sink_b = jnp.broadcast_to(sink.astype(jnp.float32).reshape(1, ATT_KV_HEADS, ATT_GROUP, 1, 1),
                              (B, ATT_KV_HEADS, ATT_GROUP, C, 1))
    p = jax.nn.softmax(jnp.concatenate([s, sink_b], axis=-1), axis=-1).astype(v_ctx.dtype)
    return jnp.einsum('bkgts,bskd->btkgd', p[..., :C], v_ctx).reshape(B, C, H * dh)

def mlstm_chunkwise(q, k, v, i_pre, f_pre, state):
    B, L, H, dqk = q.shape
    dv = v.shape[-1]
    T = ML_CHUNK
    nc = L // T

    def chunks(a):
        return a.astype(jnp.float32).reshape(B, nc, T, *a.shape[2:]).swapaxes(0, 1)

    qs, vs = chunks(q), chunks(v)
    ks = chunks(k) * (dqk ** -0.5)
    i_s = chunks(i_pre)
    lf_s = jax.nn.log_sigmoid(chunks(f_pre))
    tril = jnp.tril(jnp.ones((T, T), dtype=bool))

    def step(carry, xs):
        Cm, n, m = carry
        qc, kc, vc, ic, lfc = xs
        b = jnp.cumsum(lfc, axis=1).transpose(0, 2, 1)
        ih = ic.transpose(0, 2, 1)
        dmat = jnp.where(tril, b[..., :, None] - b[..., None, :] + ih[..., None, :], -jnp.inf)
        inter = b + m[..., None]
        m_t = jnp.maximum(inter, dmat.max(axis=-1))
        s = jnp.einsum('bthd,bshd->bhts', qc, kc) * jnp.exp(dmat - m_t[..., None])
        w_inter = jnp.exp(inter - m_t)
        num = (jnp.einsum('bhts,bshv->bthv', s, vc)
               + jnp.einsum('bthd,bhdv->bthv', qc, Cm) * w_inter.transpose(0, 2, 1)[..., None])
        nq = s.sum(axis=-1) + w_inter * jnp.einsum('bthd,bhd->bht', qc, n)
        den = jnp.maximum(jnp.abs(nq), jnp.exp(-m_t))
        h = num / den.transpose(0, 2, 1)[..., None]
        b_last = b[..., -1]
        a = b_last[..., None] - b + ih
        m_new = jnp.maximum(b_last + m, a.max(axis=-1))
        wk = jnp.exp(a - m_new[..., None]).transpose(0, 2, 1)[..., None]
        decay = jnp.exp(b_last + m - m_new)
        C_new = decay[..., None, None] * Cm + jnp.einsum('bshd,bshv->bhdv', kc * wk, vc)
        n_new = decay[..., None] * n + jnp.einsum('bshd->bhd', kc * wk)
        return (C_new, n_new, m_new), h

    state, hs = lax.scan(step, state, (qs, ks, vs, i_s, lf_s))
    return hs.swapaxes(0, 1).reshape(B, L, H, dv), state

def mlstm_bidirectional(q, k, v, g, q_c, k_c, v_c, g_c):
    B = q.shape[0]
    init = (jnp.zeros((B, ML_HEADS, ML_QK_DIM, ML_V_DIM), jnp.float32),
            jnp.zeros((B, ML_HEADS, ML_QK_DIM), jnp.float32),
            jnp.zeros((B, ML_HEADS), jnp.float32))

    def fl(a):
        return jnp.flip(a, axis=1)

    hc_f, st_f = mlstm_chunkwise(q_c, k_c, v_c, g_c[:, :, 0, 0], g_c[:, :, 0, 1], init)
    hc_b, st_b = mlstm_chunkwise(fl(q_c), fl(k_c), fl(v_c), fl(g_c[:, :, 1, 0]), fl(g_c[:, :, 1, 1]), init)
    h_f, _ = mlstm_chunkwise(q, k, v, g[:, :, 0, 0], g[:, :, 0, 1], st_f)
    h_b, _ = mlstm_chunkwise(fl(q), fl(k), fl(v), fl(g[:, :, 1, 0]), fl(g[:, :, 1, 1]), st_b)
    return h_f + fl(h_b), hc_f + fl(hc_b)

def mlstm_readout(h_tilde, o_pre, norm_w):
    B, L = h_tilde.shape[:2]
    hn = rms_norm(h_tilde, norm_w.reshape(ML_HEADS, ML_V_DIM)).reshape(B, L, ML_V_W)
    return hn.astype(o_pre.dtype) * jax.nn.sigmoid(o_pre)

def merge_branches(att, ml, ga_pre, gm_pre, w_branch_att, w_branch_ml, w_out):
    y = jax.nn.sigmoid(ga_pre) * (att @ w_branch_att) + jax.nn.sigmoid(gm_pre) * (ml @ w_branch_ml)
    return y @ w_out

def conv_ffn(h, w_up, conv_w, conv_b, w_down):
    L = h.shape[1]
    u = h @ w_up
    r = CONV_W // 2
    up = jnp.pad(u, ((0, 0), (r, r), (0, 0)))
    acc = conv_b
    for j in range(CONV_W):
        acc = acc + up[:, j:j + L] * conv_w[j]
    a, g = jnp.split(acc, 2, axis=-1)
    return (jax.nn.silu(g) * a) @ w_down

def second_inputs(seed: int = 0) -> dict:
    key = jax.random.key(seed)
    ks = jax.random.split(key, 24)
    f32 = jnp.float32

    def nrm(k, shape, scale):
        return jax.random.normal(k, shape, f32) * scale

    gate_offset = jnp.array([0.0, 3.0], f32).reshape(1, 1, 2, 1)
    return {
        "x": nrm(ks[0], (BATCH, SEQ, D_MODEL), 1.0),
        "c": nrm(ks[1], (BATCH, D_MODEL), 1.0),
        "ctx": nrm(ks[2], (BATCH, CTX_LEN, D_MODEL), 1.0),
        "c_ctx": nrm(ks[3], (D_MODEL,), 1.0),
        "w_mod": nrm(ks[4], (DEPTH, D_MODEL, 6 * D_MODEL), 0.5 * D_MODEL ** -0.5),
        "b_mod": nrm(ks[5], (DEPTH, 6 * D_MODEL), 0.02),
        "norm1_w": 1.0 + nrm(ks[6], (DEPTH, D_MODEL), 0.02),
        "w_in": nrm(ks[7], (DEPTH, D_MODEL, IN_W), D_MODEL ** -0.5),
        "q_norm_w": 1.0 + nrm(ks[8], (DEPTH, ATT_HEAD_DIM), 0.02),
        "k_norm_w": 1.0 + nrm(ks[9], (DEPTH, ATT_HEAD_DIM), 0.02),
        "attn_sink": nrm(ks[10], (DEPTH, ATT_HEADS), 0.5),
        "ml_gate_b": gate_offset + nrm(ks[11], (DEPTH, 2, 2, ML_HEADS), 0.3),
        "ml_norm_w": 1.0 + nrm(ks[12], (DEPTH, ML_V_W), 0.02),
        "w_branch_att": nrm(ks[13], (DEPTH, ATT_Q_W, D_MODEL), ATT_Q_W ** -0.5),
        "w_branch_ml": nrm(ks[14], (DEPTH, ML_V_W, D_MODEL), ML_V_W ** -0.5),
        "w_out": nrm(ks[15], (DEPTH, D_MODEL, D_MODEL), D_MODEL ** -0.5),
        "norm2_w": 1.0 + nrm(ks[16], (DEPTH, D_MODEL), 0.02),
        "w_up": nrm(ks[17], (DEPTH, D_MODEL, 2 * D_FF), D_MODEL ** -0.5),
        "conv_w": nrm(ks[18], (DEPTH, CONV_W, 2 * D_FF), CONV_W ** -0.5),
        "conv_b": nrm(ks[19], (DEPTH, 2 * D_FF), 0.02),
        "w_down": nrm(ks[20], (DEPTH, D_FF, D_MODEL), D_FF ** -0.5),
    }

def second_block(x, c, ctx, c_ctx, w_mod, b_mod, norm1_w, w_in, q_norm_w, k_norm_w, attn_sink,
              ml_gate_b, ml_norm_w, w_branch_att, w_branch_ml, w_out, norm2_w, w_up, conv_w, conv_b, w_down):
    B, L, _ = x.shape
    C = ctx.shape[1]
    rows = L // GRID_W
    cos, sin = axial_rope(rows)
    for l in range(DEPTH):
        mod = jax.nn.silu(c) @ w_mod[l] + b_mod[l]
        mod_c = jax.nn.silu(c_ctx)[None, :] @ w_mod[l] + b_mod[l]
        sh1, sc1, g1, sh2, sc2, g2 = jnp.split(mod, 6, axis=-1)
        sh1c, sc1c, g1c, sh2c, sc2c, g2c = jnp.split(mod_c, 6, axis=-1)

        h = modulate(rms_norm(x, norm1_w[l]), sh1, sc1)
        hc = modulate(rms_norm(ctx, norm1_w[l]), sh1c, sc1c)
        aq, ak, av, mq, mk, mv, mo, mg, ga, gm = split_in_proj(h @ w_in[l])
        aqc, akc, avc, mqc, mkc, mvc, moc, mgc, gac, gmc = split_in_proj(hc @ w_in[l])

        q = apply_rope(rms_norm(heads(aq, ATT_HEADS, ATT_HEAD_DIM), q_norm_w[l]), cos, sin)
        k = apply_rope(rms_norm(heads(ak, ATT_KV_HEADS, ATT_HEAD_DIM), k_norm_w[l]), cos, sin)
        v = heads(av, ATT_KV_HEADS, ATT_HEAD_DIM)
        k_ctx = rms_norm(heads(akc, ATT_KV_HEADS, ATT_HEAD_DIM), k_norm_w[l])
        v_ctx = heads(avc, ATT_KV_HEADS, ATT_HEAD_DIM)
        att = windowed_gqa(q, k, v, k_ctx, v_ctx, attn_sink[l])

        gates = mg.reshape(B, L, 2, 2, ML_HEADS) + ml_gate_b[l]
        gates_c = mgc.reshape(B, C, 2, 2, ML_HEADS) + ml_gate_b[l]
        ht, ht_c = mlstm_bidirectional(
            heads(mq, ML_HEADS, ML_QK_DIM), heads(mk, ML_HEADS, ML_QK_DIM), heads(mv, ML_HEADS, ML_V_DIM), gates,
            heads(mqc, ML_HEADS, ML_QK_DIM), heads(mkc, ML_HEADS, ML_QK_DIM), heads(mvc, ML_HEADS, ML_V_DIM), gates_c)
        ml = mlstm_readout(ht, mo, ml_norm_w[l])

        y = merge_branches(att, ml, ga, gm, w_branch_att[l], w_branch_ml[l], w_out[l])
        x_mid = x + g1[:, None, :] * y

        if l < DEPTH - 1:
            q_c = rms_norm(heads(aqc, ATT_HEADS, ATT_HEAD_DIM), q_norm_w[l])
            att_c = context_gqa(q_c, k_ctx, v_ctx, attn_sink[l])
            ml_c = mlstm_readout(ht_c, moc, ml_norm_w[l])
            y_c = merge_branches(att_c, ml_c, gac, gmc, w_branch_att[l], w_branch_ml[l], w_out[l])
            ctx = ctx + g1c[:, None, :] * y_c
            ctx = ctx + g2c[:, None, :] * conv_ffn(modulate(rms_norm(ctx, norm2_w[l]), sh2c, sc2c),
                                                   w_up[l], conv_w[l], conv_b[l], w_down[l])

        x = x_mid + g2[:, None, :] * conv_ffn(modulate(rms_norm(x_mid, norm2_w[l]), sh2, sc2),
                                              w_up[l], conv_w[l], conv_b[l], w_down[l])
    return x


def setup_inputs(seed=0):
    out = dict(first_inputs(seed))
    for name, value in second_inputs(seed + 1).items():
        if name != "x":
            out[name + "_2"] = value
    return out


def reference(
    x, norm_mix, w_in, ssd_conv_w, ssd_conv_b, dt_bias, a_log, d_skip, ssd_norm, sc_conv_w,
    sc_norm, w_out, norm_ffn, w_router_group, w_router_expert, w_gate, w_up, w_down, final_norm,
    c_2, ctx_2, c_ctx_2, w_mod_2, b_mod_2, norm1_w_2, w_in_2, q_norm_w_2, k_norm_w_2,
    attn_sink_2, ml_gate_b_2, ml_norm_w_2, w_branch_att_2, w_branch_ml_2, w_out_2, norm2_w_2,
    w_up_2, conv_w_2, conv_b_2, w_down_2,
):
    x = first_block(
        x, norm_mix, w_in, ssd_conv_w, ssd_conv_b, dt_bias, a_log, d_skip, ssd_norm, sc_conv_w,
        sc_norm, w_out, norm_ffn, w_router_group, w_router_expert, w_gate, w_up, w_down,
        final_norm,
    )
    return second_block(
        x, c_2, ctx_2, c_ctx_2, w_mod_2, b_mod_2, norm1_w_2, w_in_2, q_norm_w_2, k_norm_w_2,
        attn_sink_2, ml_gate_b_2, ml_norm_w_2, w_branch_att_2, w_branch_ml_2, w_out_2,
        norm2_w_2, w_up_2, conv_w_2, conv_b_2, w_down_2,
    )


_drawn_inputs = setup_inputs


def setup_inputs(seed=0):
    import zlib

    import numpy as np

    out = dict(_drawn_inputs(seed))
    spreads = {}
    factors = {'ssd_conv_b': 3.81,
     'ssd_norm': 2.984,
     'final_norm': 2.77,
     'ctx_2': 3.579,
     'b_mod_2': 2.816,
     'norm1_w_2': 8.0,
     'q_norm_w_2': 8.0,
     'k_norm_w_2': 8.0,
     'attn_sink_2': 8.0,
     'ml_norm_w_2': 49.777,
     'norm2_w_2': 8.0,
     'conv_b_2': 8.0}
    for name, (base, spread) in spreads.items():
        noise = np.random.default_rng([zlib.crc32(name.encode()), seed]).standard_normal(out[name].shape)
        drawn = base * np.exp(spread * noise) if base else spread * noise
        out[name] = jnp.asarray(drawn.astype(out[name].dtype))
    for name, factor in factors.items():
        out[name] = (out[name] * factor).astype(out[name].dtype)
    return out
```

```python
import math

import numpy as np

import concourse.bass as bass
from concourse import mybir

F32 = mybir.dt.float32
I32 = mybir.dt.int32
U32 = mybir.dt.uint32
ACT = mybir.ActivationFunctionType
ALU = mybir.AluOpType
AX = mybir.AxisListType

P = 128
BANK = 512
D = 1024
KT = D // P
SEQ = 512
TT = SEQ // P
EPS = 1e-6
NEG = -1e30

SSD_W, CONV_CH, HEADS, HD, STATE, GROUPS, HPG = 1024, 1536, 16, 64, 128, 2, 8
SSD_TAPS, SC_TAPS, SC_GROUP = 4, 3, 64
COL_Z, COL_XBC, COL_DT, COL_B, COL_C, COL_V = 0, 1024, 2560, 2576, 3600, 4624
NG, EPG, NE, FF, TOPK = 4, 8, 32, 512, 2
PAIRS = SEQ * TOPK
ROWS = 64
OVER = PAIRS // ROWS - 1
IOTA = PAIRS + ROWS
CTX = 256
CT = CTX // P
AH, KVH, DH = 16, 4, 64
MH, QK, DV = 4, 128, 256
DFF = 2816
FT = DFF // P
C2_Q, C2_KV, C2_MQ, C2_MK, C2_MV, C2_MO, C2_MG, C2_GA, C2_GM = 0, 1024, 1536, 2048, 2560, 3584, 4608, 4624, 5648

VEC_ROWS = [
    [("norm_mix", 8), ("ssd_norm", 8), ("sc_norm", 8), ("sc_conv_w", 24), ("ssd_conv_w", 48), ("ssd_conv_b", 12),
     ("final_norm", 8)],
    [("norm1_w_2", 8), ("norm2_w_2", 8), ("ml_norm_w_2", 8), ("b_mod_2", 48), ("conv_b_2", 44)],
    [("conv_w_2a", 88)],
    [("conv_w_2b", 44)],
]
VEC = {}
for _i, _rows in enumerate(VEC_ROWS):
    _at = _i * P
    for _name, _n in _rows:
        VEC[_name] = _at
        _at += _n

SLOTS = 6
SLOT = 4096
ARENA = 26652
SET = 44


def shape_constants():
    i = np.arange(P)
    eye = np.eye(P, dtype=np.float32)
    upto = (i[:, None] <= i[None, :]).astype(np.float32)
    before = (i[:, None] < i[None, :]).astype(np.float32)
    ones = np.ones((P, P), np.float32)
    group = (i[:, None] // SC_GROUP == i[None, :] // SC_GROUP).astype(np.float32)
    mask_le = np.where(i[None, :] <= i[:, None], 0, NEG).astype(np.float32)
    mask_ge = np.where(i[None, :] >= i[:, None], 0, NEG).astype(np.float32)
    mats = np.stack([eye, ones, upto, before, group, mask_le, mask_ge, upto.T], 1)
    pos = np.arange(SEQ)
    freq = (10000.0 ** (-np.arange(DH // 4, dtype=np.float32) / (DH // 4))).astype(np.float32)
    ang = np.concatenate([(pos // 64)[:, None].astype(np.float32) * freq,
                          (pos % 64)[:, None].astype(np.float32) * freq], -1)
    rope = np.stack([np.cos(ang), np.sin(ang)], 1).astype(np.float32)
    iota = np.zeros((P, IOTA + 1), np.float32)
    iota[:, :IOTA] = np.arange(IOTA)
    iota[:, IOTA] = i + 1
    return {"k_mats": mats.reshape(P, -1), "k_rope": rope.reshape(SEQ, -1), "k_iota": iota}


def after(c, name):
    key = c.key(name)
    c.counts[key] = c.counts.get(key, 0) + 1
    return c.counts[key]


class Core:

    def __init__(self, nc, dram):
        self.nc, self.dram = nc, dram
        self.ring = nc.alloc_sbuf_tensor("weight_ring", [P, SLOTS * SLOT], F32)
        self.arena = nc.alloc_sbuf_tensor("arena", [P, ARENA], F32)
        self.mats = nc.alloc_sbuf_tensor("mats", [P, 8, P], F32)
        self.ident, self.ones, self.upto, self.before, self.group, self.mask_le, self.mask_ge, self.since = (
            self.mats[:, i, :] for i in range(8))
        self.vec = nc.alloc_sbuf_tensor("vec", [P, (len(VEC_ROWS) - 1) * P + 44], F32)
        self.mod = nc.alloc_sbuf_tensor("mod", [P, 48, 2], F32)
        self.small = nc.alloc_sbuf_tensor("small", [P, 300], F32)
        self.ints = nc.alloc_sbuf_tensor("ints", [P, 88], I32)
        self.eps = self.small[:, 0:1]
        self.one = self.small[:, 1:2]
        self.norm_ffn = self.small[:, 2:10]
        self.ss = self.small[:, 10:26]
        self.rs = self.small[:, 26:42]
        self.gates = self.small[:, 240:248].rearrange("p (t j) -> p t j", t=TT)
        self.rowf = self.small[:, 282:290].rearrange("p (t j) -> p t j", t=TT)
        self.starts = self.ints[0:1, 0:NE + 1]
        self.over_expert = self.ints[0:1, 33:33 + OVER]
        self.over_row = self.ints[0:1, 49:49 + OVER]
        self.over_count = self.ints[0:1, 65:66]
        self.rows = self.ints[:, 66:66 + 2 * TT]
        self.psum = nc.alloc_psum_tensor("psum", [P, 8, BANK], F32)
        self.sems, self.used, self.stage, self.lasting = {}, {}, 0, set()
        self.lasting.update(("stored", "y_stored0", "y_stored1", "over_stored"))
        self.counts = {}
        self.open_sets()
        self.loads, self.turn, self.building = {}, 0, None
        self.used_slot, self.holder = [0] * SLOTS, [None] * SLOTS

    def key(self, name):
        if name.startswith(("slot_loaded", "stage_done", "gathered", "x_again")) or name in self.lasting \
                or name.endswith(("_step", "_loaded")):
            return name
        return self.stage, name

    def sem(self, name):
        key = self.key(name)
        if key == name and key not in self.sems:
            self.sems[key] = self.nc.alloc_semaphore(name)
        if key not in self.sems:
            pool = self.sets[self.stage % 2]
            self.used[self.stage] = self.used.get(self.stage, 0) + 1
            self.sems[key] = pool[self.used[self.stage] - 1]
        return self.sems[key]

    def open_sets(self):
        self.sets = [[self.nc.alloc_semaphore(f"stage_set{i}_{j}") for j in range(SET)] for i in range(2)]

    def clear(self, pool, stage):
        nums = [x.num for x in self.sets[stage % 2]]
        assert nums == list(range(nums[0], nums[0] + SET))
        pool.sem_clear(range(nums[0], nums[0] + SET)).then_inc(self.sem("clear_step"), 1)
        pool.wait_ge(self.sem("clear_step"), stage + 1)

    def at(self, start, *shape):
        n = int(np.prod(shape))
        assert start + n <= ARENA
        v = self.arena[:, start:start + n]
        if len(shape) == 2:
            v = v.rearrange("p (a b) -> p a b", a=shape[0])
        if len(shape) == 3:
            v = v.rearrange("p (a b c) -> p a b c", a=shape[0], b=shape[1])
        return v

    def ext(self, start, *shape):
        n = int(np.prod(shape))
        assert start + n <= 2 * SLOT
        v = self.ring[:, 4 * SLOT + start:4 * SLOT + start + n]
        if len(shape) == 2:
            v = v.rearrange("p (a b) -> p a b", a=shape[0])
        if len(shape) == 3:
            v = v.rearrange("p (a b c) -> p a b c", a=shape[0], b=shape[1])
        return v

    def v(self, name, tile):
        return self.vec[:, VEC[name] + tile:VEC[name] + tile + 1]

    def plan(self, key, src, kt, width, freed, slots=SLOTS, stage=None):
        self.turn = self.turn if self.turn < slots else 0
        slot = self.turn
        self.loads[key] = {"src": src, "kt": kt, "width": width, "slot": slot, "use": self.used_slot[slot],
                           "holder": self.holder[slot], "stage": stage, "of": self.building}
        self.used_slot[slot] += 1
        self.holder[slot] = freed
        self.lasting.add(freed[0])
        self.turn = (slot + 1) % slots

    def slot(self, s, kt, width):
        return self.ring[:, s * SLOT:s * SLOT + kt * width].rearrange("p (k n) -> p k n", k=kt)

    def weights(self, pe, key):
        x = self.loads[key]
        pe.wait_ge(self.sem(f"slot_loaded{x['slot']}"), 16 * (x["use"] + 1))
        return self.slot(x["slot"], x["kt"], x["width"])

    def barrier(self, eng, n):
        eng.drain().then_inc(self.sem("stage_done"), 1)
        eng.wait_ge(self.sem("stage_done"), 4 * n)
        eng.drain()


class Stage:

    def __init__(self, c):
        self.c = c

    def sync(self, eng):
        c = self.c
        for x in c.loads.values():
            if x["of"] != type(self).__name__:
                continue
            if x["stage"] is not None:
                eng.wait_ge(c.sem("stage_done"), 4 * (x["stage"] + 1))
            if x["holder"]:
                eng.wait_ge(c.sem(x["holder"][0]), x["holder"][1])
            eng.dma_start(c.slot(x["slot"], x["kt"], x["width"]), x["src"]) \
               .then_inc(c.sem(f"slot_loaded{x['slot']}"), 16)

    def pool(self, eng):
        pass

    def act(self, eng):
        pass


A0, A1, A2, A3, A4 = 0, 4096, 8192, 14336, 22528
B_X, B_H, B_ATT, B_HC, B_V, B_KT, B_QT, B_WORK = 0, 4096, 8192, 12288, 14336, 15872, 18944, 23040
B_VM, B_KTOK, B_QMT, B_T, B_ML, B_Y = 14336, 20504, 23576, 25624, 14336, 18432
B_ACT, B_FT = 8192, 19456


def rms_tokens(c, eng, n_tiles, src, junk, width, first=0):
    for t in range(n_tiles):
        eng.activation(junk, src(t), ACT.Square, accum_out=c.ss[:, first + t:first + t + 1]) \
           .then_inc(c.sem("act_step"), 1)
        eng.wait_ge(c.sem("act_step"), after(c, "act_step"))
    eng.activation(c.rs[:, first:first + n_tiles], c.ss[:, first:first + n_tiles], ACT.Sqrt, scale=1.0 / width,
                   bias=c.eps).then_inc(c.sem("act_step"), 1)
    eng.wait_ge(c.sem("act_step"), after(c, "act_step"))


def invert(c, eng, x):
    eng.reciprocal(x, x).then_inc(c.sem("dve_step"), 1)
    eng.wait_ge(c.sem("dve_step"), after(c, "dve_step"))


class Normalise1(Stage):

    def __init__(self, c):
        self.c = c
        self.x = c.at(A0, TT, D)
        self.xn = c.at(A3, TT, D)
        self.ht = c.at(A1, KT, SEQ)
        self.rows = [c.at(A4 + i * P, P) for i in range(4)]

    def pool(self, eng):
        c = self.c
        eng.memset(c.eps, EPS).then_inc(c.sem("pool_step"), 1)
        eng.wait_ge(c.sem("pool_step"), after(c, "pool_step"))
        eng.memset(c.one, 1.0).then_inc(c.sem("pool_step"), 1)
        eng.wait_ge(c.sem("pool_step"), after(c, "pool_step"))

    def sync(self, eng):
        c, d = self.c, self.c.dram
        xv = d["x"].rearrange("(t p) d -> p t d", p=P)
        for t in range(TT):
            eng.dma_start(self.x[:, t, :], xv[:, t, :]).then_inc(c.sem(f"x_loaded{t}"), 16)
        const = c.sem("const_loaded")
        eng.dma_start(c.mats[:, :, :], d["k_mats"].rearrange("p (m n) -> p m n", n=P)).then_inc(const, 16)
        for i, rows in enumerate(VEC_ROWS):
            at = 0
            for name, n in rows:
                src = d[name[:-1] if name.startswith("conv_w_2") else name]
                if name.startswith("conv_w_2"):
                    taps = src.rearrange("k (f n) -> k f n", n=P)
                    for j, k in enumerate([0, 1] if name[-1] == "a" else [2]):
                        eng.dma_start(self.rows[i][at + 44 * j:at + 44 * j + 44, :], taps[k]).then_inc(const, 16)
                    continue
                if len(src.shape) == 2:
                    src = src.rearrange("k n -> (k n)")
                eng.dma_start(self.rows[i][at:at + n, :], src.rearrange("(f n) -> f n", n=P)).then_inc(const, 16)
                at += n
        eng.dma_start(c.norm_ffn, d["norm_ffn"].rearrange("(p k) -> p k", k=KT)).then_inc(const, 16)
        eng.wait_ge(const, 16 * (2 + sum(len(r) for r in VEC_ROWS) + 1))

    def act(self, eng):
        c = self.c
        for t in range(TT):
            eng.wait_ge(c.sem(f"x_loaded{t}"), 16)
            if t == 0:
                eng.wait_ge(c.sem("pool_step"), 2)
            eng.activation(self.c.at(A2, D), self.x[:, t, :], ACT.Square, accum_out=c.ss[:, t:t + 1]) \
               .then_inc(c.sem("act_step"), 1)
            eng.wait_ge(c.sem("act_step"), after(c, "act_step"))
        eng.activation(c.rs[:, 0:TT], c.ss[:, 0:TT], ACT.Sqrt, scale=1.0 / D, bias=c.eps).then_inc(c.sem("n1_rs"), 1)
        for k in range(KT):
            eng.wait_ge(c.sem("n1_turned"), k + 1)
            if k == 0:
                eng.wait_ge(c.sem("vec_ready"), len(VEC_ROWS))
            eng.activation(self.ht[:, k, :], c.psum[:, k % 2, :], ACT.Copy, scale=c.v("norm_mix", k)) \
               .then_inc(c.sem("n1_taken"), 1)

    def dve(self, eng):
        c = self.c
        eng.wait_ge(c.sem("vec_turned"), 1)
        for i, rows in enumerate(VEC_ROWS):
            n = sum(r[1] for r in rows)
            ins = eng.tensor_copy(c.vec[:, i * P:i * P + n], c.psum[:, 7, i * P:i * P + n])
            ins.then_inc(c.sem("vec_ready"), 1)
        eng.wait_ge(c.sem("n1_rs"), 1)
        invert(c, eng, c.rs[:, 0:TT])
        for t in range(TT):
            eng.tensor_scalar(self.xn[:, t, :], self.x[:, t, :], c.rs[:, t:t + 1], None, ALU.mult) \
               .then_inc(c.sem("n1_scaled"), 1)

    def pe(self, eng):
        c = self.c
        eng.wait_ge(c.sem("const_loaded"), 16 * (2 + sum(len(r) for r in VEC_ROWS) + 1))
        for i, rows in enumerate(VEC_ROWS):
            n = sum(r[1] for r in rows)
            ins = eng.transpose(c.psum[:, 7, i * P:i * P + n], self.rows[i][0:n, :], c.ident[0:n, 0:n])
        ins.then_inc(c.sem("vec_turned"), 1)
        eng.wait_ge(c.sem("n1_scaled"), TT)
        for k in range(KT):
            if k >= 2:
                eng.wait_ge(c.sem("n1_taken"), k - 1)
            for t in range(TT):
                ins = eng.transpose(c.psum[:, k % 2, t * P:(t + 1) * P], self.xn[:, t, k * P:(k + 1) * P], c.ident)
            ins.then_inc(c.sem("n1_turned"), 1)


def feature_tile(eng, out, w, col, rhs, kt=KT):
    for k in range(kt):
        ins = eng.matmul(out, w[:, k, col:col + P], rhs[:, k, :], start=k == 0, stop=k == kt - 1)
    return ins


def token_tile(eng, out, lhs, t, w, first=True, last=True, kt=KT):
    for k in range(kt):
        ins = eng.matmul(out, lhs[:, k, t * P:(t + 1) * P], w[:, k, :], start=first and k == 0,
                         stop=last and k == kt - 1)
    return ins


class Project1(Stage):

    def __init__(self, c):
        self.c = c
        w = c.dram["w_in"].rearrange("(k p) n -> p k n", p=P)
        for i in range(3):
            c.plan(("xbc", i), w[:, :, COL_XBC + 512 * i:COL_XBC + 512 * (i + 1)], KT, 512,
                   ("xbc_made", 4 * (i + 1)))
        for i in range(2):
            for name, col in (("c", COL_C), ("v", COL_V), ("b", COL_B)):
                c.plan((name, i), w[:, :, col + 512 * i:col + 512 * (i + 1)], KT, 512,
                       (f"sc_{name}_made", 4 * (i + 1)))
        for i in range(2):
            c.plan(("z", i), w[:, :, COL_Z + 512 * i:COL_Z + 512 * (i + 1)], KT, 512,
                   ("z_made", 4 * (i + 1)))
        self.ht = c.at(A1, KT, SEQ)
        self.xbc = c.at(A2, 12, SEQ)
        self.sc = c.at(A3 + 8 * SEQ, 8, SEQ)
        self.z = c.at(A0, TT, D)
        self.conv = [c.at(A4 + i * 512, 512) for i in range(2)]
        self.cc = [c.at(A4 + 1024 + i * 512, 512) for i in range(2)]
        self.cv = c.at(A4 + 2048, 512)
        self.cu = c.at(A4 + 2560, 512)
        self.sq = c.at(A4 + 2048, 512)
        self.wdt = c.small[:, 42:170].rearrange("p (k n) -> p k n", k=KT)
        self.dt = c.small[:, 170:234].rearrange("p (t h) -> p t h", t=TT)

    def pool(self, eng):
        c = self.c
        wdt = c.dram["w_in"].rearrange("(k p) n -> p k n", p=P)[:, :, COL_DT:COL_DT + HEADS]
        eng.dma_start(self.wdt, wdt).then_inc(c.sem("wdt_loaded"), 16)

    def pe(self, eng):
        c = self.c
        for f in range(12):
            w = c.weights(eng, ("xbc", f // 4))
            if f >= 2:
                eng.wait_ge(c.sem("xbc_taken"), f - 1)
            ins = feature_tile(eng, c.psum[:, f % 2, :], w, f % 4 * P, self.ht)
            ins.then_inc(c.sem("xbc_made"), 1)
        for j in range(8):
            for name, bank in (("c", 2), ("v", 4), ("b", 6)):
                w = c.weights(eng, (name, j // 4))
                if j >= 2:
                    eng.wait_ge(c.sem(f"sc_{name}_taken"), j - 1)
                ins = feature_tile(eng, c.psum[:, bank + j % 2, :], w, j % 4 * P, self.ht)
                ins.then_inc(c.sem(f"sc_{name}_made"), 1)
        eng.wait_ge(c.sem("xbc_taken"), 12)
        for h in range(2):
            w = c.weights(eng, ("z", h))
            for t in range(TT):
                n = h * TT + t
                if n >= 2:
                    eng.wait_ge(c.sem("z_taken"), n - 1)
                ins = token_tile(eng, c.psum[:, n % 2, :], self.ht, t, w)
                ins.then_inc(c.sem("z_made"), 1)
        eng.wait_ge(c.sem("sc_c_taken"), 8)
        eng.wait_ge(c.sem("wdt_loaded"), 16)
        for t in range(TT):
            ins = token_tile(eng, c.psum[:, 2, t * HEADS:(t + 1) * HEADS], self.ht, t, self.wdt)
        ins.then_inc(c.sem("dt_made"), 1)
        for j in range(8):
            eng.wait_ge(c.sem("sc_squared"), j + 1)
            if j == 0:
                eng.wait_ge(c.sem("sc_v_taken"), 8)
            if j >= 2:
                eng.wait_ge(c.sem("sc_rs"), j - 1)
            eng.matmul(c.psum[:, 4 + j % 2, :], c.group, self.sq2(j), start=True, stop=True) \
               .then_inc(c.sem("sc_summed"), 1)

    def sq2(self, j):
        return self.c.at(A4 + 2048 + 512 * (j % 2), 512)

    def act(self, eng):
        c = self.c
        for f in range(12):
            eng.wait_ge(c.sem("xbc_conv"), f + 1)
            eng.activation(self.xbc[:, f, :], self.conv[f % 2], ACT.Silu).then_inc(c.sem("xbc_silu"), 1)
        for j in range(8):
            eng.wait_ge(c.sem("sc_c_made"), j + 1)
            if j >= 2:
                eng.wait_ge(c.sem("sc_v_taken"), j - 1)
            eng.activation(self.cc[j % 2], c.psum[:, 2 + j % 2, :], ACT.Copy).then_inc(c.sem("sc_c_taken"), 1)
        for n in range(2 * TT):
            h, t = n // TT, n % TT
            eng.wait_ge(c.sem("z_made"), n + 1)
            eng.activation(self.z[:, t, h * 512:(h + 1) * 512], c.psum[:, n % 2, :], ACT.Silu) \
               .then_inc(c.sem("z_taken"), 1)
        eng.wait_ge(c.sem("sc_b_taken"), 8)
        for j in range(8):
            if j >= 2:
                eng.wait_ge(c.sem("sc_summed"), j - 1)
            eng.activation(self.sq2(j), self.sc[:, j, :], ACT.Square).then_inc(c.sem("sc_squared"), 1)
            eng.wait_ge(c.sem("sc_summed"), j + 1)
            if j >= 2:
                eng.wait_ge(c.sem("sc_scaled"), j - 1)
            eng.activation(self.cc[j % 2], c.psum[:, 4 + j % 2, :], ACT.Ln, scale=1.0 / SC_GROUP,
                           bias=c.eps).then_inc(c.sem("act_step"), 1)
            eng.wait_ge(c.sem("act_step"), after(c, "act_step"))
            eng.activation(self.cc[j % 2], self.cc[j % 2], ACT.Exp, scale=-0.5).then_inc(c.sem("sc_rs"), 1)

    def dve(self, eng):
        c = self.c
        for f in range(12):
            eng.wait_ge(c.sem("xbc_made"), f + 1)
            if f >= 2:
                eng.wait_ge(c.sem("xbc_silu"), f - 1)
            p, a = c.psum[:, f % 2, :], self.conv[f % 2]
            eng.tensor_scalar(a, p, c.v("ssd_conv_w", 36 + f), c.v("ssd_conv_b", f), ALU.mult, ALU.add) \
               .then_inc(c.sem("dve_step"), 1)
            eng.wait_ge(c.sem("dve_step"), after(c, "dve_step"))
            for back in (1, 2):
                eng.scalar_tensor_tensor(a[:, back:], p[:, :SEQ - back], c.v("ssd_conv_w", 36 - 12 * back + f),
                                         a[:, back:], ALU.mult, ALU.add).then_inc(c.sem("dve_step"), 1)
                eng.wait_ge(c.sem("dve_step"), after(c, "dve_step"))
            eng.scalar_tensor_tensor(a[:, 3:], p[:, :SEQ - 3], c.v("ssd_conv_w", f), a[:, 3:], ALU.mult,
                                     ALU.add).then_inc(c.sem("xbc_taken"), 1)
            eng.wait_ge(c.sem("xbc_taken"), after(c, "xbc_taken"))
            eng.sem_inc(c.sem("xbc_conv"), 1)
        for j in range(8):
            eng.wait_ge(c.sem("sc_c_taken"), j + 1)
            eng.wait_ge(c.sem("sc_v_made"), j + 1)
            eng.tensor_tensor(self.cv, self.cc[j % 2], c.psum[:, 4 + j % 2, :], ALU.mult) \
               .then_inc(c.sem("sc_v_taken"), 1)
            eng.wait_ge(c.sem("sc_v_taken"), after(c, "sc_v_taken"))
            eng.tensor_scalar(self.cu, self.cv, c.v("sc_conv_w", 16 + j), None, ALU.mult) \
               .then_inc(c.sem("dve_step"), 1)
            eng.wait_ge(c.sem("dve_step"), after(c, "dve_step"))
            for back in (1, 2):
                eng.scalar_tensor_tensor(self.cu[:, back:], self.cv[:, :SEQ - back],
                                         c.v("sc_conv_w", 16 - 8 * back + j), self.cu[:, back:],
                                         ALU.mult, ALU.add).then_inc(c.sem("dve_step"), 1)
                eng.wait_ge(c.sem("dve_step"), after(c, "dve_step"))
            eng.wait_ge(c.sem("sc_b_made"), j + 1)
            eng.tensor_tensor(self.sc[:, j, :], self.cu, c.psum[:, 6 + j % 2, :], ALU.mult) \
               .then_inc(c.sem("sc_b_taken"), 1)
            eng.wait_ge(c.sem("sc_b_taken"), after(c, "sc_b_taken"))
        eng.wait_ge(c.sem("dt_made"), 1)
        eng.tensor_copy(self.dt, c.psum[:, 2, 0:TT * HEADS].rearrange("p (t h) -> p t h", t=TT)) \
           .then_inc(c.sem("dve_step"), 1)
        eng.wait_ge(c.sem("dve_step"), after(c, "dve_step"))
        for j in range(8):
            eng.wait_ge(c.sem("sc_rs"), j + 1)
            eng.scalar_tensor_tensor(self.sc[:, j, :], self.sc[:, j, :], c.v("sc_norm", j), self.cc[j % 2],
                                     ALU.mult, ALU.mult).then_inc(c.sem("sc_scaled"), 1)
            eng.wait_ge(c.sem("sc_scaled"), after(c, "sc_scaled"))


class Modulation:

    def __init__(self, c):
        self.c = c
        w = c.dram["w_mod_2"].rearrange("(p k) n -> p k n", k=KT)
        for i in range(12):
            c.plan(("mod", i), w[:, :, i * 512:(i + 1) * 512], KT, 512, ("mod_made", i // 4 + 1))
        self.raw = c.small[:, 42:58].rearrange("p (w k) -> p w k", w=2)
        self.cs = c.small[:, 58:74].rearrange("p (k w) -> p k w", w=2)
        self.rows = c.at(A4 + 3584, 512)

    def pool(self, eng):
        c = self.c
        eng.dma_start(self.raw[:, 0, :], c.dram["c_2"].rearrange("(p k) -> p k", k=KT)).then_inc(c.sem("c_loaded"), 16)
        eng.dma_start(self.raw[:, 1, :], c.dram["c_ctx_2"].rearrange("(p k) -> p k", k=KT)) \
           .then_inc(c.sem("c_loaded"), 16)
        eng.memset(self.rows, 0.0).then_inc(c.sem("mod_zero"), 1)
        eng.wait_ge(c.sem("mod_zero"), after(c, "mod_zero"))

    def act(self, eng):
        c = self.c
        eng.wait_ge(c.sem("c_loaded"), 32)
        eng.activation(self.cs, self.raw.rearrange("p w k -> p k w"), ACT.Silu).then_inc(c.sem("cs_made"), 1)

    def products(self, eng, m, half):
        c = self.c
        if m == 0 and half == 0:
            eng.wait_ge(c.sem("cs_made"), 1)
            eng.wait_ge(c.sem("xt_taken"), 2 * TT)
        if m >= 1 and half == 0:
            eng.wait_ge(c.sem("mod_rows"), 4 * m)
        w = [c.weights(eng, ("mod", 4 * m + j)) for j in range(4)]
        for k in range(KT // 2 * half, KT // 2 * (half + 1)):
            for j in range(4):
                ins = eng.matmul(c.psum[32 * j:32 * j + 2, 6, :], self.cs[:, k, :], w[j][:, k, :], start=k == 0,
                                 stop=k == KT - 1, tile_position=(0, 32 * j))
        if half == 1:
            ins.then_inc(c.sem("mod_made"), 1)

    def take(self, eng, m):
        c = self.c
        eng.wait_ge(c.sem("mod_made"), m + 1)
        eng.wait_ge(c.sem("mod_zero"), 1)
        if m >= 1:
            eng.wait_ge(c.sem("mod_turned"), m)
        for j in range(4):
            eng.activation(self.rows[32 * j:32 * j + 2, :], c.psum[32 * j:32 * j + 2, 6, :], ACT.Copy) \
               .then_inc(c.sem("mod_rows"), 1)
            eng.wait_ge(c.sem("mod_rows"), after(c, "mod_rows"))

    def turn(self, eng, m):
        c = self.c
        eng.wait_ge(c.sem("mod_rows"), 4 * (m + 1))
        if m >= 1:
            eng.wait_ge(c.sem("mod_added"), m)
        for q in range(4):
            ins = eng.transpose(c.psum[:, 7, q * P:(q + 1) * P], self.rows[:, q * P:(q + 1) * P], c.ident)
        ins.then_inc(c.sem("mod_turned"), 1)

    def add(self, eng, m):
        c = self.c
        eng.wait_ge(c.sem("mod_turned"), m + 1)
        b = VEC["b_mod_2"]
        part = c.mod[:, 16 * m:16 * (m + 1), :].rearrange("p (j q) w -> p j q w", j=4)
        src = c.psum[:, 7, :].rearrange("p (q j r) -> p j q r", q=4, j=4)[:, :, :, 0:2]
        bias = c.vec[:, b + 16 * m:b + 16 * (m + 1)].rearrange("p (j q) -> p j q", j=4)
        eng.tensor_tensor(part[:, :, :, 0], src[:, :, :, 0], bias, ALU.add).then_inc(c.sem("dve_step"), 1)
        eng.wait_ge(c.sem("dve_step"), after(c, "dve_step"))
        eng.tensor_tensor(part[:, :, :, 1], src[:, :, :, 1], bias, ALU.add).then_inc(c.sem("mod_added"), 1)
        eng.wait_ge(c.sem("mod_added"), after(c, "mod_added"))


class Scan1(Stage):

    def __init__(self, c):
        self.c = c
        self.xbc = c.at(A2, 12, SEQ)
        self.xt = c.at(A1, TT, D)
        self.z = c.at(A0, TT, D)
        self.out = c.at(A3, 8, SEQ)
        self.dt = c.small[:, 170:234].rearrange("p (t h) -> p t h", t=TT)
        self.bt = c.at(A3, TT, 256)
        self.decay = [c.at(A3 + 1024 + 1024 * i, HPG, P) for i in range(2)]
        self.xdt = c.at(A3 + 3072, 512)
        self.xw = c.at(A3 + 3584, 512)
        self.state = c.at(A4, GROUPS, 512)
        self.tmp = c.at(A4 + 1024, 512)
        self.yy = [c.at(A2 + 512 * i, 512) for i in range(2)]
        self.cbm = c.at(A4 + 2048, P)
        b = A4 + 2176
        names = ["bias", "alog", "dskip", "dta", "ac", "eac", "aend", "dec", "dte", "u1", "u2"]
        self.t = {}
        for n in names:
            k = 1 if n in ("bias", "alog", "dskip") else TT
            self.t[n] = c.at(b, k, HEADS) if k > 1 else c.at(b, HEADS)
            b += k * HEADS
        self.junk = c.at(A4 + 3072, 512)
        self.modulation = Modulation(c)

    def pool(self, eng):
        c, d = self.c, self.c.dram
        self.modulation.pool(eng)
        for name, src in (("bias", "dt_bias"), ("alog", "a_log"), ("dskip", "d_skip")):
            eng.dma_start(self.t[name], d[src].rearrange("(a n) -> a n", a=1).to_broadcast([P, HEADS])) \
               .then_inc(c.sem("head_loaded"), 16)
        eng.memset(self.state, 0.0).then_inc(c.sem("state_zero"), 1)
        eng.wait_ge(c.sem("state_zero"), after(c, "state_zero"))
        eng.wait_ge(c.sem("scan_ready"), 1)
        eng.wait_ge(c.sem("xt_taken"), 2 * TT)
        for n in range(TT * GROUPS):
            t, g = n // GROUPS, n % GROUPS
            x = self.split(self.xt[:, t, g * 512:(g + 1) * 512])
            if n >= 1:
                eng.wait_ge(c.sem("state_made"), n)
            eng.tensor_tensor(self.split(self.xw), x, self.heads(self.t["dte"], t, g), ALU.mult) \
               .then_inc(c.sem("xw_made"), 1)
            eng.wait_ge(c.sem("xw_made"), after(c, "xw_made"))
            if n >= 1:
                eng.wait_ge(c.sem("y_made"), n)
            eng.tensor_tensor(self.split(self.xdt), x, self.heads(self.dt, t, g), ALU.mult) \
               .then_inc(c.sem("xdt_made"), 1)
            eng.wait_ge(c.sem("xdt_made"), after(c, "xdt_made"))
            if n >= 1:
                eng.wait_ge(c.sem("skip_taken"), n)
            eng.tensor_tensor(self.split(self.tmp), x, self.t["dskip"][:, g * HPG:(g + 1) * HPG].unsqueeze(2)
                              .to_broadcast([P, HPG, HD]), ALU.mult).then_inc(c.sem("skip_made"), 1)
            eng.wait_ge(c.sem("skip_made"), after(c, "skip_made"))
            if n >= 1:
                self.gate(eng, n - 1)
        self.gate(eng, TT * GROUPS - 1)

    def gate(self, eng, n):
        c = self.c
        t, g = n // GROUPS, n % GROUPS
        eng.wait_ge(c.sem("y_taken"), n + 1)
        z = self.z[:, t, g * 512:(g + 1) * 512]
        eng.tensor_tensor(z, z, self.yy[n % 2], ALU.mult).then_inc(c.sem("gated"), 1)
        eng.wait_ge(c.sem("gated"), after(c, "gated"))

    def heads(self, a, t, g):
        return a[:, t, g * HPG:(g + 1) * HPG].unsqueeze(2).to_broadcast([P, HPG, HD])

    def split(self, a):
        return a.rearrange("p (h d) -> p h d", h=HPG)

    def pe(self, eng):
        c = self.c
        for t in range(TT):
            tok = slice(t * P, (t + 1) * P)
            for half in range(2):
                n = 2 * t + half
                if n >= 2:
                    eng.wait_ge(c.sem("xt_taken"), n - 1)
                for f in range(4):
                    ins = eng.transpose(c.psum[:, 6 + half, f * P:(f + 1) * P], self.xbc[:, half * 4 + f, tok], c.ident)
                ins.then_inc(c.sem("xt_turned"), 1)
        for t in range(TT):
            for g in range(2):
                ins = eng.transpose(c.psum[:, 2 + t // 2, (t % 2 * 2 + g) * P:(t % 2 * 2 + g + 1) * P],
                                    self.xbc[:, 8 + g, t * P:(t + 1) * P], c.ident)
        ins.then_inc(c.sem("bt_turned"), 1)
        eng.wait_ge(c.sem("dta_ready"), 1)
        for t in range(TT):
            ins = eng.matmul(c.psum[:, 4, t * HEADS:(t + 1) * HEADS], c.upto, self.t["dta"][:, t, :], start=True,
                             stop=True)
        ins.then_inc(c.sem("ac_made"), 1)
        for t in range(TT):
            ins = eng.matmul(c.psum[:, 5, t * HEADS:(t + 1) * HEADS], c.ones, self.t["dta"][:, t, :], start=True,
                             stop=True)
        ins.then_inc(c.sem("aend_made"), 1)
        eng.wait_ge(c.sem("scan_ready"), 1)
        self.sums(eng, 0)
        for t in range(TT):
            tok = slice(t * P, (t + 1) * P)
            for g in range(GROUPS):
                n = t * GROUPS + g
                if n >= 1:
                    eng.wait_ge(c.sem("cb_taken"), n)
                eng.matmul(c.psum[:, 2, 0:P], self.xbc[:, 8 + g, tok], self.xbc[:, 10 + g, tok], start=True,
                           stop=True).then_inc(c.sem("cb_made"), 1)
                if n >= 1:
                    eng.wait_ge(c.sem("off_taken"), n)
                if n >= GROUPS:
                    eng.wait_ge(c.sem("state_done"), n - GROUPS + 1)
                else:
                    eng.wait_ge(c.sem("state_zero"), 1)
                eng.matmul(c.psum[:, 4, :], self.xbc[:, 10 + g, tok], self.state[:, g, :], start=True,
                           stop=True).then_inc(c.sem("off_made"), 1)
                eng.wait_ge(c.sem("xw_made"), n + 1)
                if n >= 1:
                    eng.wait_ge(c.sem("state_done"), n)
                eng.matmul(c.psum[:, 5, :], self.bt[:, t, g * P:(g + 1) * P], self.xw, start=True,
                           stop=True).then_inc(c.sem("state_made"), 1)
                if n + 1 < TT * GROUPS:
                    self.sums(eng, n + 1)
                if n < 6:
                    self.modulation.products(eng, n // 2, n % 2)
                if n in (2, 4, 6):
                    self.modulation.turn(eng, n // 2 - 1)
                eng.wait_ge(c.sem("mix_made"), n + 1)
                eng.wait_ge(c.sem("xdt_made"), n + 1)
                if n >= 1:
                    eng.wait_ge(c.sem("y_taken"), n)
                for h in range(HPG):
                    ins = eng.matmul(c.psum[:, 3, h * HD:(h + 1) * HD], self.decay[n % 2][:, h, :],
                                     self.xdt[:, h * HD:(h + 1) * HD], start=True, stop=True)
                ins.then_inc(c.sem("y_made"), 1)
        eng.wait_ge(c.sem("gated_scaled"), 1)
        for f in range(8):
            if f >= 2:
                eng.wait_ge(c.sem("ssd_taken"), f - 1)
            for t in range(TT):
                ins = eng.transpose(c.psum[:, 6 + f % 2, t * P:(t + 1) * P], self.z[:, t, f * P:(f + 1) * P], c.ident)
            ins.then_inc(c.sem("ssd_turned"), 1)

    def sums(self, eng, n):
        c = self.c
        t, g = n // GROUPS, n % GROUPS
        if n >= 1:
            eng.wait_ge(c.sem("sums_taken"), n)
        for h in range(HPG):
            ins = eng.matmul(c.psum[:, h // 4, h % 4 * P:(h % 4 + 1) * P],
                             self.t["dta"][:, t, g * HPG + h:g * HPG + h + 1].to_broadcast([P, P]),
                             c.upto, start=True, stop=True)
        ins.then_inc(c.sem("sums_made"), 1)

    def act(self, eng):
        c, q = self.c, self.t
        for n in range(2 * TT):
            eng.wait_ge(c.sem("xt_turned"), n + 1)
            eng.activation(self.xt[:, n // 2, n % 2 * 512:(n % 2 + 1) * 512], c.psum[:, 6 + n % 2, :],
                           ACT.Copy).then_inc(c.sem("xt_taken"), 1)
            eng.wait_ge(c.sem("xt_taken"), after(c, "xt_taken"))
        eng.wait_ge(c.sem("bt_turned"), 1)
        eng.activation(self.bt, c.psum[:, 2:4, :].rearrange("p b (t n) -> p (b t) n", t=2), ACT.Copy) \
           .then_inc(c.sem("act_step"), 1)
        eng.wait_ge(c.sem("act_step"), after(c, "act_step"))
        self.modulation.act(eng)
        eng.wait_ge(c.sem("head_loaded"), 48)
        eng.activation(q["alog"], q["alog"], ACT.Exp).then_inc(c.sem("a_exp"), 1)
        eng.wait_ge(c.sem("a_exp"), after(c, "a_exp"))
        eng.wait_ge(c.sem("dt_split"), 1)
        eng.activation(q["u2"], q["u2"], ACT.Exp).then_inc(c.sem("act_step"), 1)
        eng.wait_ge(c.sem("act_step"), after(c, "act_step"))
        eng.activation(q["u2"], q["u2"], ACT.Ln, bias=c.one).then_inc(c.sem("dt_log"), 1)
        eng.wait_ge(c.sem("dt_log"), after(c, "dt_log"))
        eng.wait_ge(c.sem("ac_copied"), 1)
        eng.activation(q["eac"], q["ac"], ACT.Exp).then_inc(c.sem("act_step"), 1)
        eng.wait_ge(c.sem("act_step"), after(c, "act_step"))
        eng.activation(q["dec"], q["aend"], ACT.Exp).then_inc(c.sem("act_step"), 1)
        eng.wait_ge(c.sem("act_step"), after(c, "act_step"))
        eng.activation(q["dte"], q["dte"], ACT.Exp).then_inc(c.sem("decays_exp"), 1)
        eng.wait_ge(c.sem("decays_exp"), after(c, "decays_exp"))
        for n in range(TT * GROUPS):
            eng.wait_ge(c.sem("seg_made"), n + 1)
            eng.activation(self.decay[n % 2], self.decay[n % 2], ACT.Exp).then_inc(c.sem("seg_exp"), 1)
            if n in (2, 4, 6):
                self.modulation.take(eng, n // 2 - 1)
            if n >= 2:
                self.square(eng, n - 2)
        self.square(eng, TT * GROUPS - 2)
        self.square(eng, TT * GROUPS - 1)
        eng.activation(c.rs[:, 0:8], c.ss[:, 0:8], ACT.Sqrt, scale=1.0 / 512, bias=c.eps).then_inc(c.sem("ssd_rs"), 1)
        eng.wait_ge(c.sem("ssd_rs"), after(c, "ssd_rs"))
        for f in range(8):
            eng.wait_ge(c.sem("ssd_turned"), f + 1)
            eng.activation(self.out[:, f, :], c.psum[:, 6 + f % 2, :], ACT.Copy, scale=c.v("ssd_norm", f)) \
               .then_inc(c.sem("ssd_taken"), 1)

    def square(self, eng, n):
        c = self.c
        t, g = n // GROUPS, n % GROUPS
        eng.wait_ge(c.sem("gated"), n + 1)
        eng.activation(self.junk, self.z[:, t, g * 512:(g + 1) * 512], ACT.Square,
                       accum_out=c.ss[:, n:n + 1]).then_inc(c.sem("act_step"), 1)
        eng.wait_ge(c.sem("act_step"), after(c, "act_step"))

    def dve(self, eng):
        c, q = self.c, self.t

        heads, split = self.heads, self.split
        eng.wait_ge(c.sem("head_loaded"), 48)
        eng.tensor_tensor(self.dt, self.dt, q["bias"].unsqueeze(1).to_broadcast([P, TT, HEADS]), ALU.add) \
           .then_inc(c.sem("dve_step"), 1)
        eng.wait_ge(c.sem("dve_step"), after(c, "dve_step"))
        eng.tensor_scalar(q["u1"], self.dt, 0.0, None, ALU.max).then_inc(c.sem("dve_step"), 1)
        eng.wait_ge(c.sem("dve_step"), after(c, "dve_step"))
        eng.tensor_scalar(q["u2"], self.dt, 0.0, None, ALU.min).then_inc(c.sem("dve_step"), 1)
        eng.wait_ge(c.sem("dve_step"), after(c, "dve_step"))
        eng.tensor_tensor(q["u2"], q["u2"], q["u1"], ALU.subtract).then_inc(c.sem("dt_split"), 1)
        eng.wait_ge(c.sem("dt_split"), after(c, "dt_split"))
        eng.wait_ge(c.sem("dt_log"), 1)
        eng.tensor_tensor(self.dt, q["u1"], q["u2"], ALU.add).then_inc(c.sem("dve_step"), 1)
        eng.wait_ge(c.sem("dve_step"), after(c, "dve_step"))
        eng.wait_ge(c.sem("a_exp"), 1)
        eng.scalar_tensor_tensor(q["dta"], self.dt, -1.0, q["alog"].unsqueeze(1).to_broadcast([P, TT, HEADS]),
                                 ALU.mult, ALU.mult).then_inc(c.sem("dta_ready"), 1)
        eng.wait_ge(c.sem("dta_ready"), after(c, "dta_ready"))
        small = lambda b: c.psum[:, b, 0:TT * HEADS].rearrange("p (t h) -> p t h", t=TT)
        eng.wait_ge(c.sem("ac_made"), 1)
        eng.tensor_copy(q["ac"], small(4)).then_inc(c.sem("dve_step"), 1)
        eng.wait_ge(c.sem("dve_step"), after(c, "dve_step"))
        eng.wait_ge(c.sem("aend_made"), 1)
        eng.tensor_copy(q["aend"], small(5)).then_inc(c.sem("dve_step"), 1)
        eng.wait_ge(c.sem("dve_step"), after(c, "dve_step"))
        eng.tensor_tensor(q["dte"], q["aend"], q["ac"], ALU.subtract).then_inc(c.sem("ac_copied"), 1)
        eng.wait_ge(c.sem("ac_copied"), after(c, "ac_copied"))
        eng.wait_ge(c.sem("decays_exp"), 1)
        eng.tensor_tensor(q["dte"], q["dte"], self.dt, ALU.mult).then_inc(c.sem("scan_ready"), 1)
        eng.wait_ge(c.sem("scan_ready"), after(c, "scan_ready"))
        eng.wait_ge(c.sem("xt_taken"), 2 * TT)
        self.segments(eng, 0)
        for n in range(TT * GROUPS):
            t, g = n // GROUPS, n % GROUPS
            seg, yy = self.decay[n % 2], self.yy[n % 2]
            eng.wait_ge(c.sem("cb_made"), n + 1)
            eng.tensor_tensor(self.cbm, c.psum[:, 2, 0:P], c.upto, ALU.mult).then_inc(c.sem("cb_taken"), 1)
            eng.wait_ge(c.sem("cb_taken"), after(c, "cb_taken"))
            eng.wait_ge(c.sem("seg_exp"), n + 1)
            eng.tensor_tensor(seg, seg, self.cbm.unsqueeze(1).to_broadcast([P, HPG, P]), ALU.mult) \
               .then_inc(c.sem("mix_made"), 1)
            eng.wait_ge(c.sem("mix_made"), after(c, "mix_made"))
            if n + 1 < TT * GROUPS:
                self.segments(eng, n + 1)
            eng.wait_ge(c.sem("off_made"), n + 1)
            eng.tensor_tensor(split(self.state[:, g, :]), split(self.state[:, g, :]), heads(q["dec"], t, g),
                              ALU.mult).then_inc(c.sem("dve_step"), 1)
            eng.wait_ge(c.sem("dve_step"), after(c, "dve_step"))
            eng.wait_ge(c.sem("state_made"), n + 1)
            eng.tensor_tensor(self.state[:, g, :], self.state[:, g, :], c.psum[:, 5, :], ALU.add) \
               .then_inc(c.sem("state_done"), 1)
            eng.wait_ge(c.sem("state_done"), after(c, "state_done"))
            if n >= 2:
                eng.wait_ge(c.sem("gated"), n - 1)
            eng.tensor_tensor(split(yy), split(c.psum[:, 4, :]), heads(q["eac"], t, g), ALU.mult) \
               .then_inc(c.sem("off_taken"), 1)
            eng.wait_ge(c.sem("off_taken"), after(c, "off_taken"))
            eng.wait_ge(c.sem("skip_made"), n + 1)
            eng.tensor_tensor(yy, yy, self.tmp, ALU.add).then_inc(c.sem("skip_taken"), 1)
            eng.wait_ge(c.sem("skip_taken"), after(c, "skip_taken"))
            eng.wait_ge(c.sem("y_made"), n + 1)
            eng.tensor_tensor(yy, yy, c.psum[:, 3, :], ALU.add).then_inc(c.sem("y_taken"), 1)
            eng.wait_ge(c.sem("y_taken"), after(c, "y_taken"))
            if n in (3, 5, 7):
                self.modulation.add(eng, (n - 3) // 2)
        eng.wait_ge(c.sem("ssd_rs"), 1)
        invert(c, eng, c.rs[:, 0:8])
        for n in range(TT * GROUPS):
            t, g = n // GROUPS, n % GROUPS
            zz = self.z[:, t, g * 512:(g + 1) * 512]
            eng.tensor_scalar(zz, zz, c.rs[:, n:n + 1], None, ALU.mult).then_inc(c.sem("dve_step"), 1)
            eng.wait_ge(c.sem("dve_step"), after(c, "dve_step"))
        eng.sem_inc(c.sem("gated_scaled"), 1)

    def segments(self, eng, n):
        c = self.c
        t, g = n // GROUPS, n % GROUPS
        seg = self.decay[n % 2]
        eng.wait_ge(c.sem("sums_made"), n + 1)
        if n >= 2:
            eng.wait_ge(c.sem("y_made"), n - 1)
        eng.tensor_tensor(seg, c.psum[:, 0:2, :].rearrange("p b (h l) -> p (b h) l", h=4),
                          self.t["ac"][:, t, g * HPG:(g + 1) * HPG].unsqueeze(2).to_broadcast([P, HPG, P]),
                          ALU.subtract).then_inc(c.sem("sums_taken"), 1)
        eng.wait_ge(c.sem("sums_taken"), after(c, "sums_taken"))
        eng.tensor_scalar(seg, seg, 0.0, None, ALU.min).then_inc(c.sem("seg_made"), 1)
        eng.wait_ge(c.sem("seg_made"), after(c, "seg_made"))


class Out1(Stage):

    def __init__(self, c):
        self.c = c
        w = c.dram["w_out"].rearrange("(k p) n -> p k n", p=P)
        for h in range(2):
            for kh in range(2):
                c.plan(("w_out", h, kh), w[:, kh * 8:(kh + 1) * 8, h * 512:(h + 1) * 512], 8, 512,
                       ("out1_made", 4 * (h + 1)))
        self.cat = c.at(A3, 16, SEQ)
        self.h1 = c.at(A1, TT, D)

    def pool(self, eng):
        c = self.c
        eng.dma_start(self.h1, c.dram["x"].rearrange("(t p) d -> p t d", p=P)).then_inc(c.sem("x_again"), 16)

    def pe(self, eng):
        c = self.c
        for h in range(2):
            w = [c.weights(eng, ("w_out", h, kh)) for kh in range(2)]
            for t in range(TT):
                out = c.psum[:, h * 4 + t, :]
                for kh in range(2):
                    ins = token_tile(eng, out, self.cat[:, kh * 8:(kh + 1) * 8, :], t, w[kh], first=kh == 0,
                                     last=kh == 1)
                ins.then_inc(c.sem("out1_made"), 1)

    def dve(self, eng):
        c = self.c
        eng.wait_ge(c.sem("x_again"), 16)
        for n in range(2 * TT):
            h, t = n // TT, n % TT
            eng.wait_ge(c.sem("out1_made"), n + 1)
            part = self.h1[:, t, h * 512:(h + 1) * 512]
            eng.tensor_tensor(part, part, c.psum[:, h * 4 + t, :], ALU.add).then_inc(c.sem("dve_step"), 1)
            eng.wait_ge(c.sem("dve_step"), after(c, "dve_step"))


class Route(Stage):

    def __init__(self, c):
        self.c = c
        self.h1 = c.at(A1, TT, D)
        self.hr = c.at(A0, TT, KT, P)
        self.hrt = c.at(A3, KT, SEQ)
        self.iota = c.at(A4, IOTA + 1)
        b = A4 + IOTA + 2
        self.wr = c.at(b, KT, NG + NE)
        b += KT * (NG + NE)
        self.t = {}
        for name, shape in (("lg", (TT, NG + NE)), ("gpad", (TT, 8)), ("gmax", (TT, 8)), ("emax", (TT, 8)),
                            ("gsel", (TT, NG)), ("gexp", (TT, NG)), ("esel", (TT, EPG)), ("prod", (TT * NG, EPG)),
                            ("gsum", (TT,)), ("d", (TT,)), ("d1", (TT,)), ("idf", (TT, 2)), ("oh0", (TT, NE)),
                            ("oh1", (TT, NE)), ("used", (TT, NE)), ("rank", (TT, NE)), ("cnt", (NE,)),
                            ("inc", (NE,)), ("start", (NE,)), ("one32", (NE,)), ("thr", (OVER,)), 
                            ("over", (NE, OVER)), ("opos", (NE, OVER)), ("cum", (NE * OVER,)), ("ocol", (2,))):
            self.t[name] = c.at(b, *shape)
            b += int(np.prod(shape))
        self.junk = c.at(A3 + 4096, NE * OVER)
        self.junk2 = c.at(A3 + 4096 + 480, NE * OVER)
        self.junk3 = c.at(A3 + 4096 + 960, NE * OVER)
        self.gidx = self.c.at(b, TT, 8).bitcast(U32)
        self.eidx = self.c.at(b + 32, TT, 8).bitcast(U32)
        assert b + 64 <= ARENA, b

    def pool(self, eng):
        c, d = self.c, self.c.dram
        eng.dma_start(self.iota, d["k_iota"]).then_inc(c.sem("iota_loaded"), 16)
        eng.dma_start(self.wr[:, :, 0:NG], d["w_router_group"].rearrange("(p k) g -> p k g", k=KT)) \
           .then_inc(c.sem("router_loaded"), 16)
        for g in range(NG):
            eng.dma_start(self.wr[:, :, NG + g * EPG:NG + (g + 1) * EPG],
                          d["w_router_expert"][g].rearrange("(p k) e -> p k e", k=KT)) \
               .then_inc(c.sem("router_loaded"), 16)
        eng.memset(self.t["gpad"], -3e38).then_inc(c.sem("route_set"), 1)
        eng.wait_ge(c.sem("route_set"), after(c, "route_set"))
        eng.memset(self.t["one32"], 1.0).then_inc(c.sem("route_set"), 1)
        eng.wait_ge(c.sem("route_set"), after(c, "route_set"))

    def pe(self, eng):
        c, q = self.c, self.t
        eng.wait_ge(c.sem("hr_made"), TT)
        for k in range(KT):
            if k >= 2:
                eng.wait_ge(c.sem("hrt_taken"), k - 1)
            for t in range(TT):
                ins = eng.transpose(c.psum[:, k % 2, t * P:(t + 1) * P], self.hr[:, t, k, :], c.ident)
            ins.then_inc(c.sem("hrt_turned"), 1)
        eng.wait_ge(c.sem("hrt_taken"), KT)
        eng.wait_ge(c.sem("router_loaded"), 16 * (1 + NG))
        for t in range(TT):
            ins = token_tile(eng, c.psum[:, 2, t * 36:(t + 1) * 36], self.hrt, t, self.wr)
        ins.then_inc(c.sem("logits_made"), 1)
        eng.wait_ge(c.sem("used_made"), 1)
        for t in range(TT):
            for j in range(t + 1):
                ins = eng.matmul(c.psum[:, 3, t * NE:(t + 1) * NE], c.before if j == t else c.ones, q["used"][:, j, :],
                                 start=j == 0, stop=j == t)
        for j in range(TT):
            ins = eng.matmul(c.psum[:, 4, 0:NE], c.ones, q["used"][:, j, :], start=j == 0, stop=j == TT - 1)
        ins.then_inc(c.sem("rank_made"), 1)
        eng.wait_ge(c.sem("ocol_made"), 1)
        for j in range(2):
            ins = eng.transpose(c.psum[0:1, 7, j * P:(j + 1) * P], q["ocol"][:, j:j + 1], c.ident)
        ins.then_inc(c.sem("orow_made"), 1)

    def act(self, eng):
        c, q = self.c, self.t
        rms_tokens(c, eng, TT, lambda t: self.h1[:, t, :], c.at(A3, D), D)
        eng.sem_inc(c.sem("h1_rs"), 1)
        for k in range(KT):
            eng.wait_ge(c.sem("hrt_turned"), k + 1)
            eng.activation(self.hrt[:, k, :], c.psum[:, k % 2, :], ACT.Copy, scale=c.norm_ffn[:, k:k + 1]) \
               .then_inc(c.sem("hrt_taken"), 1)
            eng.wait_ge(c.sem("hrt_taken"), after(c, "hrt_taken"))
        eng.wait_ge(c.sem("gdiff_made"), 1)
        eng.activation(q["gexp"], q["gexp"], ACT.Exp).then_inc(c.sem("gexp_made"), 1)
        eng.wait_ge(c.sem("gexp_made"), after(c, "gexp_made"))
        eng.wait_ge(c.sem("ediff_made"), 1)
        eng.activation(q["d"], q["d"], ACT.Exp).then_inc(c.sem("eexp_made"), 1)
        eng.wait_ge(c.sem("eexp_made"), after(c, "eexp_made"))

    def dve(self, eng):
        c, q = self.c, self.t
        eng.wait_ge(c.sem("h1_rs"), 1)
        invert(c, eng, c.rs[:, 0:TT])
        for t in range(TT):
            eng.tensor_scalar(self.hr[:, t, :, :], self.h1[:, t, :].rearrange("p (q k) -> p k q", k=KT),
                              c.rs[:, t:t + 1], None, ALU.mult).then_inc(c.sem("hr_made"), 1)
            eng.wait_ge(c.sem("hr_made"), after(c, "hr_made"))
        eng.wait_ge(c.sem("logits_made"), 1)
        eng.wait_ge(c.sem("route_set"), 2)
        eng.tensor_copy(q["lg"], c.psum[:, 2, 0:TT * 36].rearrange("p (t n) -> p t n", t=TT)) \
           .then_inc(c.sem("dve_step"), 1)
        eng.wait_ge(c.sem("dve_step"), after(c, "dve_step"))
        gl = q["lg"][:, :, 0:NG]
        eng.tensor_copy(q["gpad"][:, :, 0:NG], gl).then_inc(c.sem("dve_step"), 1)
        eng.wait_ge(c.sem("dve_step"), after(c, "dve_step"))
        for t in range(TT):
            eng.max(q["gmax"][:, t, :], q["gpad"][:, t, :]).then_inc(c.sem("dve_step"), 1)
            eng.wait_ge(c.sem("dve_step"), after(c, "dve_step"))
            eng.max_index(self.gidx[:, t, :], q["gmax"][:, t, :], q["gpad"][:, t, :]).then_inc(c.sem("dve_step"), 1)
            eng.wait_ge(c.sem("dve_step"), after(c, "dve_step"))
        eng.tensor_tensor(q["gexp"], gl, q["gmax"][:, :, 0:1].to_broadcast([P, TT, NG]), ALU.subtract) \
           .then_inc(c.sem("gdiff_made"), 1)
        eng.wait_ge(c.sem("gdiff_made"), after(c, "gdiff_made"))
        eng.tensor_copy(q["idf"][:, :, 0:1], self.gidx[:, :, 0:1]).then_inc(c.sem("dve_step"), 1)
        eng.wait_ge(c.sem("dve_step"), after(c, "dve_step"))
        eng.wait_ge(c.sem("iota_loaded"), 16)
        eng.tensor_tensor(q["gsel"], self.iota[:, 0:NG].unsqueeze(1).to_broadcast([P, TT, NG]),
                          q["idf"][:, :, 0:1].to_broadcast([P, TT, NG]), ALU.is_equal).then_inc(c.sem("dve_step"), 1)
        eng.wait_ge(c.sem("dve_step"), after(c, "dve_step"))
        el = q["lg"][:, :, NG:].rearrange("p t (g e) -> p t g e", g=NG)
        prod = q["prod"].rearrange("p (t g) e -> p t g e", t=TT)
        for t in range(TT):
            eng.tensor_tensor(prod[:, t], el[:, t], q["gsel"][:, t, :].unsqueeze(2)
                              .to_broadcast([P, NG, EPG]), ALU.mult).then_inc(c.sem("dve_step"), 1)
            eng.wait_ge(c.sem("dve_step"), after(c, "dve_step"))
        eng.tensor_reduce(q["esel"], prod.rearrange("p t g e -> p t e g"), AX.X, ALU.add) \
           .then_inc(c.sem("dve_step"), 1)
        eng.wait_ge(c.sem("dve_step"), after(c, "dve_step"))
        for t in range(TT):
            eng.max(q["emax"][:, t, :], q["esel"][:, t, :]).then_inc(c.sem("dve_step"), 1)
            eng.wait_ge(c.sem("dve_step"), after(c, "dve_step"))
            eng.max_index(self.eidx[:, t, :], q["emax"][:, t, :], q["esel"][:, t, :]).then_inc(c.sem("dve_step"), 1)
            eng.wait_ge(c.sem("dve_step"), after(c, "dve_step"))
        eng.tensor_tensor(q["d"].unsqueeze(2), q["emax"][:, :, 1:2], q["emax"][:, :, 0:1], ALU.subtract) \
           .then_inc(c.sem("ediff_made"), 1)
        eng.wait_ge(c.sem("ediff_made"), after(c, "ediff_made"))
        eng.wait_ge(c.sem("gexp_made"), 1)
        eng.tensor_reduce(q["gsum"], q["gexp"], AX.X, ALU.add).then_inc(c.sem("dve_step"), 1)
        eng.wait_ge(c.sem("dve_step"), after(c, "dve_step"))
        eng.wait_ge(c.sem("eexp_made"), 1)
        eng.tensor_scalar(q["d1"], q["d"], 1.0, None, ALU.add).then_inc(c.sem("dve_step"), 1)
        eng.wait_ge(c.sem("dve_step"), after(c, "dve_step"))
        eng.tensor_tensor(q["d1"], q["d1"], q["gsum"], ALU.mult).then_inc(c.sem("dve_step"), 1)
        eng.wait_ge(c.sem("dve_step"), after(c, "dve_step"))
        eng.reciprocal(c.gates[:, :, 0], q["d1"]).then_inc(c.sem("dve_step"), 1)
        eng.wait_ge(c.sem("dve_step"), after(c, "dve_step"))
        eng.tensor_tensor(c.gates[:, :, 1], c.gates[:, :, 0], q["d"], ALU.mult).then_inc(c.sem("dve_step"), 1)
        eng.wait_ge(c.sem("dve_step"), after(c, "dve_step"))
        eng.tensor_scalar(q["idf"][:, :, 0:1], q["idf"][:, :, 0:1], float(EPG), None, ALU.mult) \
           .then_inc(c.sem("dve_step"), 1)
        eng.wait_ge(c.sem("dve_step"), after(c, "dve_step"))
        eng.tensor_copy(q["gsum"].unsqueeze(2), q["idf"][:, :, 0:1]).then_inc(c.sem("dve_step"), 1)
        eng.wait_ge(c.sem("dve_step"), after(c, "dve_step"))
        eng.tensor_copy(q["idf"], self.eidx[:, :, 0:2]).then_inc(c.sem("dve_step"), 1)
        eng.wait_ge(c.sem("dve_step"), after(c, "dve_step"))
        eng.tensor_tensor(q["idf"], q["idf"], q["gsum"].unsqueeze(2).to_broadcast([P, TT, 2]), ALU.add) \
           .then_inc(c.sem("dve_step"), 1)
        eng.wait_ge(c.sem("dve_step"), after(c, "dve_step"))
        for j, oh in enumerate(("oh0", "oh1")):
            eng.tensor_tensor(q[oh], self.iota[:, 0:NE].unsqueeze(1).to_broadcast([P, TT, NE]),
                              q["idf"][:, :, j:j + 1].to_broadcast([P, TT, NE]), ALU.is_equal) \
               .then_inc(c.sem("dve_step"), 1)
            eng.wait_ge(c.sem("dve_step"), after(c, "dve_step"))
        eng.tensor_tensor(q["used"], q["oh0"], q["oh1"], ALU.add).then_inc(c.sem("used_made"), 1)
        eng.wait_ge(c.sem("used_made"), after(c, "used_made"))
        eng.wait_ge(c.sem("rank_made"), 1)
        eng.tensor_copy(q["cnt"], c.psum[:, 4, 0:NE]).then_inc(c.sem("dve_step"), 1)
        eng.wait_ge(c.sem("dve_step"), after(c, "dve_step"))
        eng.tensor_tensor_scan(q["inc"], q["one32"], q["cnt"], 0.0, ALU.mult, ALU.add).then_inc(c.sem("dve_step"), 1)
        eng.wait_ge(c.sem("dve_step"), after(c, "dve_step"))
        eng.tensor_tensor(q["start"], q["inc"], q["cnt"], ALU.subtract).then_inc(c.sem("dve_step"), 1)
        eng.wait_ge(c.sem("dve_step"), after(c, "dve_step"))
        eng.tensor_tensor(q["rank"], c.psum[:, 3, 0:TT * NE].rearrange("p (t n) -> p t n", t=TT),
                          q["start"].unsqueeze(1).to_broadcast([P, TT, NE]), ALU.add).then_inc(c.sem("dve_step"), 1)
        eng.wait_ge(c.sem("dve_step"), after(c, "dve_step"))
        for j, oh in enumerate(("oh0", "oh1")):
            eng.tensor_tensor(q[oh], q[oh], q["rank"], ALU.mult).then_inc(c.sem("dve_step"), 1)
            eng.wait_ge(c.sem("dve_step"), after(c, "dve_step"))
            eng.tensor_reduce(c.rowf[:, :, j], q[oh], AX.X, ALU.add).then_inc(c.sem("dve_step"), 1)
            eng.wait_ge(c.sem("dve_step"), after(c, "dve_step"))
        eng.tensor_copy(c.rows, c.rowf.rearrange("p t j -> p (t j)")).then_inc(c.sem("dve_step"), 1)
        eng.wait_ge(c.sem("dve_step"), after(c, "dve_step"))
        eng.tensor_copy(c.starts[:, 1:], q["inc"][0:1, :]).then_inc(c.sem("dve_step"), 1)
        eng.wait_ge(c.sem("dve_step"), after(c, "dve_step"))
        eng.memset(c.starts[:, 0:1], 0).then_inc(c.sem("dve_step"), 1)
        eng.wait_ge(c.sem("dve_step"), after(c, "dve_step"))
        eng.tensor_scalar(q["thr"], self.iota[:, 1:1 + OVER], float(ROWS), None, ALU.mult) \
           .then_inc(c.sem("dve_step"), 1)
        eng.wait_ge(c.sem("dve_step"), after(c, "dve_step"))
        thr = q["thr"].unsqueeze(1).to_broadcast([P, NE, OVER])
        eng.tensor_tensor(q["over"], q["cnt"].unsqueeze(2).to_broadcast([P, NE, OVER]), thr, ALU.is_gt) \
           .then_inc(c.sem("dve_step"), 1)
        eng.wait_ge(c.sem("dve_step"), after(c, "dve_step"))
        eng.tensor_tensor(q["opos"], q["start"].unsqueeze(2).to_broadcast([P, NE, OVER]), thr, ALU.add) \
           .then_inc(c.sem("dve_step"), 1)
        eng.wait_ge(c.sem("dve_step"), after(c, "dve_step"))
        flags = q["over"].rearrange("p e k -> p (e k)")
        eng.memset(self.junk, 1.0).then_inc(c.sem("dve_step"), 1)
        eng.wait_ge(c.sem("dve_step"), after(c, "dve_step"))
        eng.tensor_tensor_scan(q["cum"], self.junk, flags, 0.0, ALU.mult, ALU.add).then_inc(c.sem("dve_step"), 1)
        eng.wait_ge(c.sem("dve_step"), after(c, "dve_step"))
        eng.tensor_copy(c.over_count, q["cum"][0:1, NE * OVER - 1:]).then_inc(c.sem("dve_step"), 1)
        eng.wait_ge(c.sem("dve_step"), after(c, "dve_step"))
        eng.scalar_tensor_tensor(self.junk, q["cum"], self.iota[:, IOTA:IOTA + 1], flags, ALU.is_equal,
                                 ALU.mult).then_inc(c.sem("dve_step"), 1)
        eng.wait_ge(c.sem("dve_step"), after(c, "dve_step"))
        eng.tensor_tensor(self.junk2, self.junk, q["opos"].rearrange("p e k -> p (e k)"), ALU.mult) \
           .then_inc(c.sem("dve_step"), 1)
        eng.wait_ge(c.sem("dve_step"), after(c, "dve_step"))
        eng.tensor_reduce(q["ocol"][:, 0:1], self.junk2, AX.X, ALU.add).then_inc(c.sem("dve_step"), 1)
        eng.wait_ge(c.sem("dve_step"), after(c, "dve_step"))
        eng.tensor_tensor(self.junk3.rearrange("p (e k) -> p e k", e=NE),
                          self.junk.rearrange("p (e k) -> p e k", e=NE),
                          self.iota[:, 0:NE].unsqueeze(2).to_broadcast([P, NE, OVER]), ALU.mult) \
           .then_inc(c.sem("dve_step"), 1)
        eng.wait_ge(c.sem("dve_step"), after(c, "dve_step"))
        eng.tensor_reduce(q["ocol"][:, 1:2], self.junk3, AX.X, ALU.add).then_inc(c.sem("ocol_made"), 1)
        eng.wait_ge(c.sem("ocol_made"), after(c, "ocol_made"))
        eng.wait_ge(c.sem("orow_made"), 1)
        eng.tensor_copy(c.over_row, c.psum[0:1, 7, 0:OVER]).then_inc(c.sem("dve_step"), 1)
        eng.wait_ge(c.sem("dve_step"), after(c, "dve_step"))
        eng.tensor_copy(c.over_expert, c.psum[0:1, 7, P:P + OVER]).then_inc(c.sem("dve_step"), 1)
        eng.wait_ge(c.sem("dve_step"), after(c, "dve_step"))


class Experts(Stage):

    HALF = FF // 2

    def __init__(self, c):
        self.c = c
        self.hr = c.at(A0, TT, KT, P)
        self.iota = c.at(A4, IOTA + 1)
        base = A2
        self.xg = [c.at(base + 512 * i, KT, ROWS) for i in range(3)]
        self.sg = [c.at(base + 1536 + 256 * i, 256) for i in range(3)]
        self.hh = [c.at(base + 2304 + 256 * i, 256) for i in range(3)]
        self.ht = [c.at(base + 3072 + 256 * i, 2, P) for i in range(3)]
        self.y = [c.at(base + 3840 + 512 * i, 512) for i in range(3)]
        self.pick = c.at(base + 5376, TT, ROWS)
        self.pick2 = c.at(base + 5632, TT, ROWS)
        self.xr = c.at(base + 5888, 512)
        self.ovw = c.at(base + 6400, 4096)
        self.bank = [(0, 2, 4, 6, 7), (1, 3, 5, 6, 7), (6, 7, 5, 0, 1)]
        self.first, self.used, self.holders = c.turn, list(c.used_slot), list(c.holder)
        for b in range(2):
            for m, part in enumerate(("gate", "up", "down")):
                slot = (self.first + 3 * b + m) % SLOTS
                c.used_slot[slot] += NE // 2
                c.holder[slot] = (f"{part}_made{b}", NE // 2 + 1)
                c.lasting.add(f"{part}_made{b}")

    def sync(self, sp):
        c, d = self.c, self.c.dram
        for h in self.holders:
            if h:
                sp.wait_ge(c.sem(h[0]), h[1])
        with sp.Fori(0, NE // 2) as i:
            for b in range(2):
                for m, part in enumerate(("gate", "up", "down")):
                    slot = (self.first + 3 * b + m) % SLOTS
                    sp.wait_ge(c.sem(f"{part}_made{b}"), i + 1)
                    if part == "down":
                        src = d["w_down"].rearrange("e (k p) n -> p (e k) n", p=P)[:, bass.ds((2 * i + b) * 4, 4), :]
                        dst = c.slot(slot, 4, D)
                    else:
                        src = d[f"w_{part}"].rearrange("e (p k) n -> (e p) k n", k=KT)[
                            bass.ds((2 * i + b) * P, P), :, :]
                        dst = c.slot(slot, KT, FF)
                    sp.dma_start(dst, src).then_inc(c.sem(f"slot_loaded{slot}"), 16)

    def slot_wait(self, pe, b, m, i):
        slot = (self.first + 3 * b + m) % SLOTS
        pe.wait_ge(self.c.sem(f"slot_loaded{slot}"), 16 * i + 16 * (self.used[slot] + 1))
        return slot

    def gather(self, pe, b, sem):
        for t in range(TT):
            for j in range(2):
                ins = pe.matmul(self.c.psum[64 * j:64 * j + 64, self.bank[b][3], :], self.pick[:, t, :],
                                self.hr[:, t, 4 * j:4 * j + 4, :].rearrange("p k n -> p (k n)"), start=t == 0,
                                stop=t == TT - 1)
        ins.then_inc(sem, 1)

    def copy_rows(self, act, b, sem):
        act.activation(self.xr, self.c.psum[:, self.bank[b][3], :], ACT.Copy).then_inc(sem, 1)

    def turn_rows(self, pe, b, sem):
        for q in range(4):
            ins = pe.transpose(self.c.psum[:, self.bank[b][4], q * P:(q + 1) * P], self.xr[:, q * P:(q + 1) * P],
                               self.c.ident)
        ins.then_inc(sem, 1)

    def up_products(self, pe, b, col, w, sem):
        out = self.c.psum
        for k in range(KT):
            for j in range(2):
                ins = pe.matmul(out[64 * j:64 * j + 64, self.bank[b][0], col:col + self.HALF],
                                self.xg[b][:, k, :], w[:, k, j * self.HALF:(j + 1) * self.HALF],
                                start=k == 0, stop=k == KT - 1)
        ins.then_inc(sem, 1)

    def turn(self, pe, b, sem):
        for q in range(2):
            ins = pe.transpose(self.c.psum[:, self.bank[b][1], q * P:(q + 1) * P],
                               self.hh[b][:, q * P:(q + 1) * P], self.c.ident)
        ins.then_inc(sem, 1)

    def down_products(self, pe, b, w, sem):
        for k in range(4):
            for j in range(2):
                ins = pe.matmul(self.c.psum[64 * j:64 * j + 64, self.bank[b][2], :],
                                self.ht[b][:, k % 2, 64 * (k // 2):64 * (k // 2) + 64], w[:, k, j * 512:(j + 1) * 512],
                                start=k == 0, stop=k == 3)
        ins.then_inc(sem, 1)

    def pe(self, eng):
        c = self.c
        for name in ("gate_made0", "gate_made1", "up_made0", "up_made1", "down_made0", "down_made1", "h_turned0",
                     "h_turned1", "over_down"):
            eng.sem_inc(c.sem(name), 1)
        n_over = eng.value_load(c.over_count, min_val=0, max_val=OVER)
        with eng.Fori(0, OVER) as i:
            with eng.If(i < n_over):
                w3 = self.ovw.rearrange("p (k n) -> p k n", k=KT)
                eng.wait_ge(c.sem("over_picked"), i + 1)
                self.gather(eng, 2, c.sem("over_gathered"))
                eng.wait_ge(c.sem("over_copied"), i + 1)
                self.turn_rows(eng, 2, c.sem("over_xt"))
                eng.wait_ge(c.sem("over_x"), i + 1)
                eng.wait_ge(c.sem("over_loaded0"), 16 * i + 16)
                self.up_products(eng, 2, 0, w3, c.sem("over_gate"))
                eng.wait_ge(c.sem("over_loaded1"), 16 * i + 16)
                self.up_products(eng, 2, 256, w3, c.sem("over_up"))
                eng.wait_ge(c.sem("over_h"), i + 1)
                self.turn(eng, 2, c.sem("over_turned"))
                eng.wait_ge(c.sem("over_ht"), i + 1)
                eng.wait_ge(c.sem("over_loaded2"), 16 * i + 16)
                self.down_products(eng, 2, self.ovw.rearrange("p (k n) -> p k n", k=4), c.sem("over_down"))
                eng.wait_ge(c.sem("over_y"), i + 1)
        eng.wait_ge(c.sem("x_picked"), 1)
        self.gather(eng, 0, c.sem("x_gathered"))
        eng.wait_ge(c.sem("x_copied"), 1)
        self.turn_rows(eng, 0, c.sem("x_turned"))
        with eng.Fori(0, NE // 2) as i:
            for b in range(2):
                eng.wait_ge(c.sem("x_ready"), 2 * i + b + 1)
                slot = self.slot_wait(eng, b, 0, i)
                self.up_products(eng, b, 0, c.slot(slot, KT, FF), c.sem(f"gate_made{b}"))
                slot = self.slot_wait(eng, b, 1, i)
                self.up_products(eng, b, 256, c.slot(slot, KT, FF), c.sem(f"up_made{b}"))
                eng.wait_ge(c.sem("x_picked"), 2 * i + b + 2)
                self.gather(eng, 1 - b, c.sem("x_gathered"))
                eng.wait_ge(c.sem(f"h_made{b}"), i + 2)
                self.turn(eng, b, c.sem(f"h_turned{b}"))
                eng.wait_ge(c.sem("x_copied"), 2 * i + b + 2)
                self.turn_rows(eng, 1 - b, c.sem("x_turned"))
                eng.wait_ge(c.sem(f"ht_taken{b}"), i + 1)
                slot = self.slot_wait(eng, b, 2, i)
                self.down_products(eng, b, c.slot(slot, 4, D), c.sem(f"down_made{b}"))

    def act(self, eng):
        c, d = self.c, self.c.dram
        n_over = eng.value_load(c.over_count, min_val=0, max_val=OVER)
        with eng.Fori(0, OVER) as i:
            with eng.If(i < n_over):
                e = eng.value_load(c.over_expert[:, bass.ds(i, 1)], min_val=0, max_val=NE - 1)
                w3 = self.ovw.rearrange("p (k n) -> p k n", k=KT)
                eng.wait_ge(c.sem("over_down"), i + 1)
                eng.dma_start(w3, d["w_gate"].rearrange("e (p k) n -> (e p) k n", k=KT)[bass.ds(e * P, P), :, :]) \
                   .then_inc(c.sem("over_loaded0"), 16)
                eng.wait_ge(c.sem("over_gathered"), i + 1)
                self.copy_rows(eng, 2, c.sem("over_copied"))
                eng.wait_ge(c.sem("over_gate"), i + 1)
                eng.dma_start(w3, d["w_up"].rearrange("e (p k) n -> (e p) k n", k=KT)[bass.ds(e * P, P), :, :]) \
                   .then_inc(c.sem("over_loaded1"), 16)
                eng.wait_ge(c.sem("over_up"), i + 1)
                eng.activation(self.sg[2], c.psum[:, 6, 0:256], ACT.Silu).then_inc(c.sem("over_silu"), 1)
                eng.dma_start(self.ovw.rearrange("p (k n) -> p k n", k=4),
                              d["w_down"].rearrange("e (k p) n -> p (e k) n", p=P)[:, bass.ds(e * 4, 4), :]) \
                   .then_inc(c.sem("over_loaded2"), 16)
        eng.wait_ge(c.sem("x_gathered"), 1)
        self.copy_rows(eng, 0, c.sem("x_copied"))
        with eng.Fori(0, NE // 2) as i:
            for b in range(2):
                eng.wait_ge(c.sem(f"up_made{b}"), i + 2)
                eng.wait_ge(c.sem(f"h_made{b}"), i + 1)
                eng.activation(self.sg[b], c.psum[:, b, 0:256], ACT.Silu).then_inc(c.sem(f"silu_made{b}"), 1)
                eng.wait_ge(c.sem("x_gathered"), 2 * i + b + 2)
                self.copy_rows(eng, 1 - b, c.sem("x_copied"))

    def dve(self, eng):
        c = self.c
        for b in range(2):
            eng.sem_inc(c.sem(f"h_made{b}"), 1)
        n_over = eng.value_load(c.over_count, min_val=0, max_val=OVER)

        def pick(row, sem):
            rows = self.iota[:, bass.ds(row, ROWS)].unsqueeze(1).to_broadcast([P, TT, ROWS])
            first, second = (c.rowf[:, :, j:j + 1].to_broadcast([P, TT, ROWS]) for j in range(2))
            eng.tensor_tensor(self.pick, rows, first, ALU.is_equal)
            eng.tensor_tensor(self.pick2, rows, second, ALU.is_equal)
            eng.drain()
            eng.tensor_tensor(self.pick, self.pick, self.pick2, ALU.add).then_inc(sem, 1)

        def scale(b, sem):
            for j in range(2):
                ins = eng.tensor_tensor(self.xg[b][:, 4 * j:4 * j + 4, :],
                                        c.psum[:, self.bank[b][4], :].rearrange("p (q j n) -> p j q n", q=4,
                                                                                j=2)[:, j],
                                        c.norm_ffn[:, 4 * j:4 * j + 4].unsqueeze(2).to_broadcast([P, 4, ROWS]),
                                        ALU.mult)
            ins.then_inc(sem, 1)

        with eng.Fori(0, OVER) as i:
            with eng.If(i < n_over):
                row = eng.value_load(c.over_row[:, bass.ds(i, 1)], min_val=0, max_val=PAIRS)
                eng.wait_ge(c.sem("over_down"), i + 1)
                pick(row, c.sem("over_picked"))
                eng.wait_ge(c.sem("over_xt"), i + 1)
                scale(2, c.sem("over_x"))
                eng.wait_ge(c.sem("over_silu"), i + 1)
                eng.tensor_tensor(self.hh[2], self.sg[2], c.psum[:, 6, 256:512], ALU.mult) \
                   .then_inc(c.sem("over_h"), 1)
                eng.wait_ge(c.sem("over_turned"), i + 1)
                eng.tensor_copy(self.ht[2], c.psum[:, 7, 0:256].rearrange("p (q n) -> p q n", q=2)) \
                   .then_inc(c.sem("over_ht"), 1)
                eng.wait_ge(c.sem("over_down"), i + 2)
                eng.wait_ge(c.sem("over_done"), i + 1)
                eng.tensor_copy(self.y[2], c.psum[:, 5, :]).then_inc(c.sem("over_y"), 1)
        first = eng.value_load(c.starts[:, 0:1], min_val=0, max_val=PAIRS)
        pick(first, c.sem("x_picked"))
        eng.wait_ge(c.sem("x_turned"), 1)
        scale(0, c.sem("x_ready"))
        with eng.Fori(0, NE // 2) as i:
            for b in range(2):
                row = eng.value_load(c.starts[:, bass.ds(2 * i + b + 1, 1)], min_val=0, max_val=PAIRS)
                pick(row, c.sem("x_picked"))
                eng.wait_ge(c.sem(f"silu_made{b}"), i + 1)
                eng.wait_ge(c.sem(f"up_made{b}"), i + 2)
                eng.wait_ge(c.sem(f"h_turned{b}"), i + 1)
                eng.tensor_tensor(self.hh[b], self.sg[b], c.psum[:, b, 256:512], ALU.mult) \
                   .then_inc(c.sem(f"h_made{b}"), 1)
                eng.wait_ge(c.sem(f"h_turned{b}"), i + 2)
                eng.wait_ge(c.sem(f"down_made{b}"), i + 1)
                eng.tensor_copy(self.ht[b], c.psum[:, 2 + b, 0:256].rearrange("p (q n) -> p q n", q=2)) \
                   .then_inc(c.sem(f"ht_taken{b}"), 1)
                eng.wait_ge(c.sem("x_turned"), 2 * i + b + 2)
                scale(1 - b, c.sem("x_ready"))
                eng.wait_ge(c.sem(f"down_made{b}"), i + 2)
                eng.wait_ge(c.sem(f"y_done{b}"), i + 1)
                eng.tensor_copy(self.y[b], c.psum[:, 4 + b, :]).then_inc(c.sem(f"y_taken{b}"), 1)

    def pool(self, eng):
        c = self.c
        ys = c.dram["y_rows"]

        def store(b, row, sem):
            for j in range(2):
                eng.dma_start(ys[bass.ds(row, ROWS), j * 512:(j + 1) * 512], self.y[b][64 * j:64 * j + 64, :]) \
                   .then_inc(sem, 16)

        for name in ("y_done0", "y_done1", "over_done"):
            eng.sem_inc(c.sem(name), 1)
        n_over = eng.value_load(c.over_count, min_val=0, max_val=OVER)
        with eng.Fori(0, OVER) as i:
            with eng.If(i < n_over):
                row = eng.value_load(c.over_row[:, bass.ds(i, 1)], min_val=0, max_val=PAIRS)
                eng.wait_ge(c.sem("over_y"), i + 1)
                store(2, row, c.sem("over_stored"))
                eng.wait_ge(c.sem("over_stored"), 32 * i + 32)
                eng.sem_inc(c.sem("over_done"), 1)
        with eng.Fori(0, NE // 2) as i:
            for b in range(2):
                row = eng.value_load(c.starts[:, bass.ds(2 * i + b, 1)], min_val=0, max_val=PAIRS)
                eng.wait_ge(c.sem(f"y_taken{b}"), i + 1)
                store(b, row, c.sem(f"y_stored{b}"))
                eng.wait_ge(c.sem(f"y_stored{b}"), 32 * i + 32)
                eng.sem_inc(c.sem(f"y_done{b}"), 1)


class Combine(Stage):

    def __init__(self, c):
        self.c = c
        self.h = c.at(A1, TT, D)
        self.g = c.at(A2, 2 * TT, D)
        self.xt = c.at(A0, KT, SEQ)
        self.junk = c.at(A2 + 2 * TT * D, D)

    def pool(self, eng):
        c = self.c
        for n in range(2 * TT):
            eng.indirect_dma_start(self.g[:, n, :], None, c.dram["y_rows"][0:PAIRS, :],
                                   bass.IndirectOffsetOnAxis(ap=c.rows[:, n:n + 1], axis=0)) \
               .then_inc(c.sem(f"gathered{n // 2}"), 16)

    def dve(self, eng):
        c = self.c
        for t in range(TT):
            eng.wait_ge(c.sem(f"gathered{t}"), 32)
            for j in range(2):
                eng.scalar_tensor_tensor(self.h[:, t, :], self.g[:, 2 * t + j, :], c.gates[:, t, j:j + 1],
                                         self.h[:, t, :], ALU.mult, ALU.add).then_inc(c.sem("h2_made"), 1)
                eng.wait_ge(c.sem("h2_made"), after(c, "h2_made"))
        eng.wait_ge(c.sem("h2_rs"), 1)
        invert(c, eng, c.rs[:, 0:TT])
        for t in range(TT):
            eng.tensor_scalar(self.h[:, t, :], self.h[:, t, :], c.rs[:, t:t + 1], None, ALU.mult) \
               .then_inc(c.sem("h2_scaled"), 1)
            eng.wait_ge(c.sem("h2_scaled"), after(c, "h2_scaled"))

    def act(self, eng):
        c = self.c
        for t in range(TT):
            eng.wait_ge(c.sem("h2_made"), 2 * t + 2)
            eng.activation(self.junk, self.h[:, t, :], ACT.Square, accum_out=c.ss[:, t:t + 1]) \
               .then_inc(c.sem("act_step"), 1)
            eng.wait_ge(c.sem("act_step"), after(c, "act_step"))
        eng.activation(c.rs[:, 0:TT], c.ss[:, 0:TT], ACT.Sqrt, scale=1.0 / D, bias=c.eps).then_inc(c.sem("h2_rs"), 1)
        eng.wait_ge(c.sem("h2_rs"), after(c, "h2_rs"))
        for k in range(KT):
            eng.wait_ge(c.sem("x2_turned"), k + 1)
            eng.activation(self.xt[:, k, :], c.psum[:, k % 2, :], ACT.Copy, scale=c.v("final_norm", k)) \
               .then_inc(c.sem("x2_taken"), 1)
            eng.wait_ge(c.sem("x2_taken"), after(c, "x2_taken"))

    def pe(self, eng):
        c = self.c
        eng.wait_ge(c.sem("h2_scaled"), TT)
        for k in range(KT):
            if k >= 2:
                eng.wait_ge(c.sem("x2_taken"), k - 1)
            for t in range(TT):
                ins = eng.transpose(c.psum[:, k % 2, t * P:(t + 1) * P], self.h[:, t, k * P:(k + 1) * P], c.ident)
            ins.then_inc(c.sem("x2_turned"), 1)


class Finish(Stage):

    def __init__(self, c):
        self.c = c
        self.xt = c.at(A0, KT, SEQ)
        self.o = c.at(A1, TT, D)

    def pe(self, eng):
        c = self.c
        for n in range(2 * TT):
            if n >= 2:
                eng.wait_ge(c.sem("fin_taken"), n - 1)
            for k in range(4):
                ins = eng.transpose(c.psum[:, n % 2, k * P:(k + 1) * P],
                                    self.xt[:, n % 2 * 4 + k, n // 2 * P:(n // 2 + 1) * P], c.ident)
            ins.then_inc(c.sem("fin_turned"), 1)

    def dve(self, eng):
        c = self.c
        for n in range(2 * TT):
            eng.wait_ge(c.sem("fin_turned"), n + 1)
            eng.tensor_copy(self.o[:, n // 2, n % 2 * 512:(n % 2 + 1) * 512], c.psum[:, n % 2, :]) \
               .then_inc(c.sem("fin_taken"), 1)
            eng.wait_ge(c.sem("fin_taken"), after(c, "fin_taken"))

    def pool(self, eng):
        c = self.c
        for t in range(TT):
            eng.wait_ge(c.sem("fin_taken"), 2 * t + 2)
            eng.dma_start(c.dram["out"].rearrange("(t p) d -> t p d", p=P)[t], self.o[:, t, :]) \
               .then_inc(c.sem("stored"), 16)
        eng.wait_ge(c.sem("stored"), 16 * TT)


MOD = {"sh1": 0, "sc1": 8, "g1": 16, "sh2": 24, "sc2": 32, "g2": 40}


class Norm2(Stage):

    tag, norm, scale, shift, ctx = "a", "norm1_w_2", "sc1", "sh1", True

    def __init__(self, c):
        self.c = c
        self.x = c.at(B_X, KT, SEQ)
        self.h = c.at(B_H, KT, SEQ)
        self.sq = [c.at(B_WORK + 512 * i, 512) for i in range(2)]
        self.rb = c.at(B_WORK + 1024, 512)
        self.xr = [c.at(B_WORK + 1536 + 512 * i, 512) for i in range(2)]
        self.coef = c.small[:, 248:264].rearrange("p (w k) -> p w k", w=2)
        self.hc = c.at(B_HC, KT, CTX)
        self.cx = c.at(B_V, CT, D)

    def n(self, name):
        return self.c.sem(f"norm_{self.tag}_{name}")

    def pool(self, eng):
        if self.ctx:
            eng.dma_start(self.cx, self.c.dram["ctx_2"].rearrange("(t p) d -> p t d", p=P)) \
               .then_inc(self.n("ctx_loaded"), 16)

    def act(self, eng):
        c = self.c
        for k in range(KT):
            if k >= 2:
                eng.wait_ge(self.n("summed"), k - 1)
            eng.activation(self.sq[k % 2], self.x[:, k, :], ACT.Square).then_inc(self.n("squared"), 1)
        eng.wait_ge(self.n("summed"), KT)
        eng.activation(self.rb, c.psum[:, 0, :], ACT.Ln, scale=1.0 / D, bias=c.eps).then_inc(c.sem("act_step"), 1)
        eng.wait_ge(c.sem("act_step"), after(c, "act_step"))
        eng.activation(self.rb, self.rb, ACT.Exp, scale=-0.5).then_inc(self.n("rs"), 1)
        eng.wait_ge(self.n("rs"), after(c, f"norm_{self.tag}_" + "rs"))
        for k in range(KT):
            eng.wait_ge(self.n("scaled"), k + 1)
            eng.activation(self.h[:, k, :], self.xr[k % 2], ACT.Identity, scale=self.coef[:, 0, k:k + 1],
                           bias=c.mod[:, MOD[self.shift] + k, 0:1]).then_inc(self.n("made"), 1)
        if self.ctx:
            eng.wait_ge(self.n("ctx_loaded"), 16)
            rms_tokens(c, eng, CT, lambda t: self.cx[:, t, :], c.at(B_QT, D), D)
            eng.sem_inc(self.n("ctx_rs"), 1)

    def pe(self, eng):
        c = self.c
        for k in range(KT):
            eng.wait_ge(self.n("squared"), k + 1)
            eng.matmul(c.psum[:, 0, :], c.ones, self.sq[k % 2], start=k == 0, stop=k == KT - 1) \
               .then_inc(self.n("summed"), 1)
        if self.ctx:
            eng.wait_ge(self.n("ctx_scaled"), CT)
            for k in range(KT):
                if k >= 2:
                    eng.wait_ge(self.n("hc_taken"), k - 1)
                for t in range(CT):
                    ins = eng.transpose(c.psum[:, 2 + k % 2, t * P:(t + 1) * P], self.cx[:, t, k * P:(k + 1) * P],
                                        c.ident)
                ins.then_inc(self.n("hc_turned"), 1)

    def dve(self, eng):
        c = self.c
        w = c.vec[:, VEC[self.norm]:VEC[self.norm] + KT]
        for which in range(2 if self.ctx else 1):
            sc = c.mod[:, MOD[self.scale]:MOD[self.scale] + KT, which]
            eng.scalar_tensor_tensor(self.coef[:, which, :], sc, 1.0, w, ALU.add, ALU.mult) \
               .then_inc(c.sem("dve_step"), 1)
            eng.wait_ge(c.sem("dve_step"), after(c, "dve_step"))
        eng.wait_ge(self.n("rs"), 1)
        for k in range(KT):
            if k >= 2:
                eng.wait_ge(self.n("made"), k - 1)
            eng.tensor_tensor(self.xr[k % 2], self.x[:, k, :], self.rb, ALU.mult).then_inc(self.n("scaled"), 1)
        if self.ctx:
            eng.wait_ge(self.n("ctx_rs"), 1)
            invert(c, eng, c.rs[:, 0:CT])
            for t in range(CT):
                eng.tensor_scalar(self.cx[:, t, :], self.cx[:, t, :], c.rs[:, t:t + 1], None, ALU.mult) \
                   .then_inc(self.n("ctx_scaled"), 1)
                eng.wait_ge(self.n("ctx_scaled"), after(c, f"norm_{self.tag}_" + "ctx_scaled"))
            for k in range(KT):
                eng.wait_ge(self.n("hc_turned"), k + 1)
                sh = MOD[self.shift] + k
                eng.tensor_scalar(self.hc[:, k, :], c.psum[:, 2 + k % 2, 0:CTX], self.coef[:, 1, k:k + 1],
                                  c.mod[:, sh, 1:2], ALU.mult, ALU.add).then_inc(self.n("hc_taken"), 1)
                eng.wait_ge(self.n("hc_taken"), after(c, f"norm_{self.tag}_" + "hc_taken"))


class Norm2Ffn(Norm2):
    tag, norm, scale, shift, ctx = "b", "norm2_w_2", "sc2", "sh2", False


class AttendIn(Stage):

    def __init__(self, c):
        self.c = c
        w = c.dram["w_in_2"].rearrange("(k p) n -> p k n", p=P)
        for i in range(2):
            c.plan(("aq", i), w[:, :, C2_Q + 512 * i:C2_Q + 512 * (i + 1)], KT, 512, ("qk_made", 4 * (i + 1)), slots=4)
        c.plan("akv", w[:, :, C2_KV:C2_KV + 512], KT, 512, ("qk_made", 14), slots=4)
        self.h, self.hc = c.at(B_H, KT, SEQ), c.at(B_HC, KT, CTX)
        self.v = c.at(B_V, 6, 256)
        self.kt = c.at(B_KT, KVH, SEQ + CTX)
        self.qt = c.at(B_QT, 8, SEQ)
        self.sq = [c.at(B_WORK + 512 * i, 512) for i in range(2)]
        self.xn = [c.at(B_WORK + 1024 + 512 * i, 512) for i in range(2)]
        self.ro = [c.at(B_WORK + 2048 + 512 * i, 512) for i in range(2)]
        self.tmp = c.at(B_WORK + 3072, 2, 256)
        self.rope = c.ext(0, TT, 2, 32)
        self.wn = c.ext(256, 2, DH)
        self.ss = c.small[:, 264:272]
        self.rs = c.small[:, 272:280]
        self.units = [("q", h, t) for h in range(2) for t in range(TT)] + [("k", 0, t) for t in range(6)]

    def pool(self, eng):
        c, d = self.c, self.c.dram
        eng.dma_start(self.rope, d["k_rope"].rearrange("(t p) (w n) -> p t w n", p=P, w=2)) \
           .then_inc(c.sem("rope_loaded"), 16)
        for i, name in enumerate(("q_norm_w_2", "k_norm_w_2")):
            eng.dma_start(self.wn[:, i, :], d[name].rearrange("(a n) -> a n", a=1).to_broadcast([P, DH])) \
               .then_inc(c.sem("rope_loaded"), 16)

    def pe(self, eng):
        c = self.c
        for n in range(len(self.units) + 1):
            if n < len(self.units):
                kind, half, t = self.units[n]
                w = c.weights(eng, ("aq", half) if kind == "q" else "akv")
                if n >= 2:
                    eng.wait_ge(c.sem("qk_taken"), n - 1)
                lhs = self.h if t < TT else self.hc
                token_tile(eng, c.psum[:, n % 2, :], lhs, t % TT, w).then_inc(c.sem("qk_made"), 1)
            if n >= 1:
                kind, half, t = self.units[n - 1]
                eng.wait_ge(c.sem("qk_roped"), n)
                if n >= 3:
                    eng.wait_ge(c.sem("qk_stored"), n - 2)
                for j in range(4):
                    ins = eng.transpose(c.psum[:, 2 + (n - 1) % 2, j * P:(j + 1) * P],
                                        self.ro[(n - 1) % 2][:, j * P:(j + 1) * P], c.ident)
                ins.then_inc(c.sem("qk_turned"), 1)

    def act(self, eng):
        c = self.c
        for n, (kind, half, t) in enumerate(self.units):
            heads = 8 if kind == "q" else KVH
            eng.wait_ge(c.sem("qk_made"), n + 1)
            if n >= 2:
                eng.wait_ge(c.sem("qk_summed"), n - 1)
            eng.activation(self.sq[n % 2][:, 0:heads * DH], c.psum[:, n % 2, 0:heads * DH], ACT.Square) \
               .then_inc(c.sem("qk_squared"), 1)
            eng.wait_ge(c.sem("qk_squared"), after(c, "qk_squared"))
            if kind == "k":
                eng.activation(self.v[:, t, :], c.psum[:, n % 2, 256:512], ACT.Copy).then_inc(c.sem("act_step"), 1)
                eng.wait_ge(c.sem("act_step"), after(c, "act_step"))
            eng.wait_ge(c.sem("qk_summed"), n + 1)
            eng.activation(self.rs[:, 0:heads], self.ss[:, 0:heads], ACT.Sqrt, scale=1.0 / DH, bias=c.eps) \
               .then_inc(c.sem("qk_rs"), 1)
            eng.wait_ge(c.sem("qk_rs"), after(c, "qk_rs"))
            if n >= 1:
                self.store(eng, n - 1)
        self.store(eng, len(self.units) - 1)

    def store(self, eng, n):
        c = self.c
        kind, half, t = self.units[n]
        eng.wait_ge(c.sem("qk_turned"), n + 1)
        tok = slice(t * P, (t + 1) * P)
        dst = self.qt[:, half * 4:half * 4 + 4, tok] if kind == "q" else self.kt[:, :, tok]
        eng.activation(dst, c.psum[:, 2 + n % 2, :].rearrange("p (a n) -> p a n", a=4), ACT.Copy) \
           .then_inc(c.sem("qk_stored"), 1)
        eng.wait_ge(c.sem("qk_stored"), after(c, "qk_stored"))

    def dve(self, eng):
        c = self.c
        eng.wait_ge(c.sem("rope_loaded"), 48)
        eng.tensor_scalar(self.wn[:, 0, :], self.wn[:, 0, :], DH ** -0.5, None, ALU.mult) \
           .then_inc(c.sem("dve_step"), 1)
        eng.wait_ge(c.sem("dve_step"), after(c, "dve_step"))
        for n, (kind, half, t) in enumerate(self.units):
            H = 8 if kind == "q" else KVH
            view = lambda a: a[:, 0:H * DH].rearrange("p (h d) -> p h d", h=H)
            eng.wait_ge(c.sem("qk_squared"), n + 1)
            if n >= 1:
                eng.wait_ge(c.sem("qk_rs"), n)
            eng.tensor_reduce(self.ss[:, 0:H], view(self.sq[n % 2]), AX.X, ALU.add).then_inc(c.sem("qk_summed"), 1)
            eng.wait_ge(c.sem("qk_summed"), after(c, "qk_summed"))
            eng.wait_ge(c.sem("qk_rs"), n + 1)
            invert(c, eng, self.rs[:, 0:H])
            x = view(self.xn[n % 2])
            eng.tensor_tensor(x, view(c.psum[:, n % 2, :]), self.rs[:, 0:H].unsqueeze(2)
                              .to_broadcast([P, H, DH]), ALU.mult).then_inc(c.sem("qk_taken"), 1)
            eng.wait_ge(c.sem("qk_taken"), after(c, "qk_taken"))
            w = self.wn[:, 0 if kind == "q" else 1, :].unsqueeze(1).to_broadcast([P, H, DH])
            eng.tensor_tensor(x, x, w, ALU.mult).then_inc(c.sem("dve_step"), 1)
            eng.wait_ge(c.sem("dve_step"), after(c, "dve_step"))
            if n >= 2:
                eng.wait_ge(c.sem("qk_turned"), n - 1)
            if t < TT:
                cos = self.rope[:, t, 0, :].unsqueeze(1).to_broadcast([P, H, 32])
                sin = self.rope[:, t, 1, :].unsqueeze(1).to_broadcast([P, H, 32])
                u = self.tmp[:, 0, 0:H * 32].rearrange("p (h d) -> p h d", h=H)
                v = self.tmp[:, 1, 0:H * 32].rearrange("p (h d) -> p h d", h=H)
                o = view(self.ro[n % 2]) if kind == "q" else view(self.sq[n % 2])
                for lo, a, b, op in ((0, cos, sin, ALU.subtract), (32, sin, cos, ALU.add)):
                    eng.tensor_tensor(u, x[:, :, 0:32], a, ALU.mult).then_inc(c.sem("dve_step"), 1)
                    eng.wait_ge(c.sem("dve_step"), after(c, "dve_step"))
                    eng.tensor_tensor(v, x[:, :, 32:64], b, ALU.mult).then_inc(c.sem("dve_step"), 1)
                    eng.wait_ge(c.sem("dve_step"), after(c, "dve_step"))
                    eng.tensor_tensor(o[:, :, lo:lo + 32], u, v, op).then_inc(c.sem("dve_step"), 1)
                    eng.wait_ge(c.sem("dve_step"), after(c, "dve_step"))
            if kind == "k":
                src = view(self.sq[n % 2]) if t < TT else x
                dup = self.ro[n % 2].rearrange("p (h w d) -> p h w d", h=KVH, w=2)
                for w in range(2):
                    eng.tensor_copy(dup[:, :, w, :], src).then_inc(c.sem("dve_step"), 1)
                    eng.wait_ge(c.sem("dve_step"), after(c, "dve_step"))
            eng.sem_inc(c.sem("qk_roped"), 1)


class Attend(Stage):

    def __init__(self, c):
        self.c = c
        self.v = c.at(B_V, 6, 256)
        self.kt = c.at(B_KT, KVH, SEQ + CTX)
        self.qt = c.at(B_QT, 8, SEQ)
        self.att = c.at(B_ATT, 8, SEQ)
        self.p = [c.at(B_WORK + 640 * i, 640) for i in range(2)]
        self.pt = [c.at(B_WORK + 1280 + 640 * i, 640) for i in range(2)]
        self.sink = c.ext(384, AH)
        self.mx = c.ext(400, 2)
        self.nm = c.ext(402, 2)
        self.sum = c.ext(404, 2)
        self.es = c.ext(406, 2)
        self.ri = c.ext(408, 2)
        self.its = [(hp, blk, hh) for hp in range(8) for blk in range(TT) for hh in range(2)]

    def geometry(self, blk):
        first = max(blk - 1, 0)
        n = min(blk + 1, TT - 1) - first + 1
        return first, n, (CTX + n * P) // 2

    def pool(self, eng):
        c = self.c
        eng.dma_start(self.sink, c.dram["attn_sink_2"].rearrange("(a n) -> a n", a=1).to_broadcast([P, AH])) \
           .then_inc(c.sem("sink_loaded"), 16)

    def scores(self, n):
        return self.c.psum[:, 2 * (n % 2):2 * (n % 2) + 2, :]

    def score(self, eng, n):
        c = self.c
        hp, blk, hh = self.its[n]
        first, nl, w = self.geometry(blk)
        rows = slice(64 * hh, 64 * hh + 64)
        if n >= 2:
            eng.wait_ge(c.sem("exp_made"), n - 1)
        q = self.qt[rows, hp, blk * P:(blk + 1) * P]
        k = self.kt[rows, hp // 2, :]
        out = self.scores(n)
        eng.matmul(out[:, 0, 0:CTX], q, k[:, SEQ:SEQ + CTX], start=True, stop=True)
        lo, a = first * P, w - CTX
        before, later = blk > 0, blk < TT - 1
        if a:
            eng.matmul(out[:, 0, CTX:w], q, k[:, lo:lo + a], start=True, stop=not before)
            if before:
                eng.matmul(out[:, 0, CTX:w], c.ident, c.mask_ge[:, 0:a], start=False, stop=True)
        ins = eng.matmul(out[:, 1, 0:w], q, k[:, lo + a:lo + nl * P], start=True, stop=False)
        if before:
            ins = eng.matmul(out[:, 1, 0:P - a], c.ident, c.mask_ge[:, a:], start=False, stop=not later)
        if later:
            ins = eng.matmul(out[:, 1, w - P:w], c.ident, c.mask_le, start=False, stop=True)
        ins.then_inc(c.sem("scores_made"), 1)

    def pe(self, eng):
        c, N = self.c, len(self.its)
        self.score(eng, 0)
        self.score(eng, 1)
        for m in range(N + 1):
            if m + 2 < N:
                self.score(eng, m + 2)
            if m < N:
                nl = self.geometry(self.its[m][1])[1]
                eng.wait_ge(c.sem("p_made"), m + 1)
                if m >= 1:
                    eng.wait_ge(c.sem("pt_taken"), m)
                for b in range(2 + nl):
                    ins = eng.transpose(c.psum[:, 4 + b // 4, b % 4 * P:(b % 4 + 1) * P],
                                        self.p[m % 2][:, b * P:(b + 1) * P], c.ident)
                ins.then_inc(c.sem("p_turned"), 1)
            if m >= 1:
                self.output(eng, m - 1)

    def output(self, eng, m):
        c = self.c
        hp, blk, hh = self.its[m]
        first, nl, w = self.geometry(blk)
        eng.wait_ge(c.sem("pt_taken"), m + 1)
        if m % 8 == 0 and m >= 16:
            eng.wait_ge(c.sem("att_taken"), m // 8 - 1)
        g = hp // 2
        tiles = [4, 5] + [first + j for j in range(nl)]
        for b, tile in enumerate(tiles):
            ins = eng.matmul(c.psum[64 * hh:64 * hh + 64, 6 + hp % 2, blk * P:(blk + 1) * P],
                             self.v[:, tile, g * DH:(g + 1) * DH], self.pt[m % 2][:, b * P:(b + 1) * P],
                             start=b == 0, stop=b == len(tiles) - 1)
        ins.then_inc(c.sem("pv_made"), 1)

    def act(self, eng):
        c, N = self.c, len(self.its)
        eng.wait_ge(c.sem("sink_loaded"), 16)
        for n in range(N + 1):
            if n < N:
                hp, blk, hh = self.its[n]
                w = self.geometry(blk)[2]
                h = 2 * hp + hh
                eng.wait_ge(c.sem("max_made"), n + 1)
                if n >= 2:
                    eng.wait_ge(c.sem("p_turned"), n - 1)
                i = n % 2
                eng.activation(self.p[i][:, 0:2 * w].rearrange("p (a n) -> p a n", a=2),
                               self.scores(n)[:, :, 0:w], ACT.Exp, bias=self.nm[:, i:i + 1],
                               accum_out=self.sum[:, i:i + 1]).then_inc(c.sem("exp_made"), 1)
                eng.wait_ge(c.sem("exp_made"), after(c, "exp_made"))
                eng.activation(self.es[:, i:i + 1], self.sink[:, h:h + 1], ACT.Exp,
                               bias=self.nm[:, i:i + 1]).then_inc(c.sem("sink_exp"), 1)
                eng.wait_ge(c.sem("sink_exp"), after(c, "sink_exp"))
            if n >= 1:
                m = n - 1
                nb = 2 + self.geometry(self.its[m][1])[1]
                eng.wait_ge(c.sem("p_turned"), m + 1)
                if m >= 2:
                    eng.wait_ge(c.sem("pv_made"), m - 1)
                eng.activation(self.pt[m % 2][:, 0:nb * P],
                               c.psum[:, 4:6, :].rearrange("p b n -> p (b n)")[:, 0:nb * P], ACT.Copy) \
                   .then_inc(c.sem("pt_taken"), 1)
                eng.wait_ge(c.sem("pt_taken"), after(c, "pt_taken"))

    def dve(self, eng):
        c, N = self.c, len(self.its)
        eng.wait_ge(c.sem("sink_loaded"), 16)

        def pair_out(hp):
            eng.wait_ge(c.sem("pv_made"), 8 * (hp + 1))
            eng.tensor_copy(self.att[:, hp, :], c.psum[:, 6 + hp % 2, :]).then_inc(c.sem("att_taken"), 1)
            eng.wait_ge(c.sem("att_taken"), after(c, "att_taken"))

        for n in range(N + 1):
            if n < N:
                hp, blk, hh = self.its[n]
                first, nl, w = self.geometry(blk)
                h, i = 2 * hp + hh, n % 2
                sc = self.scores(n)
                eng.wait_ge(c.sem("scores_made"), n + 1)
                eng.tensor_reduce(self.mx[:, i:i + 1], sc[:, :, 0:w], AX.XY, ALU.max).then_inc(c.sem("dve_step"), 1)
                eng.wait_ge(c.sem("dve_step"), after(c, "dve_step"))
                if n >= 2:
                    eng.wait_ge(c.sem("sink_exp"), n - 1)
                eng.tensor_scalar(self.nm[:, i:i + 1], self.mx[:, i:i + 1], self.sink[:, h:h + 1], -1.0,
                                  ALU.max, ALU.mult).then_inc(c.sem("max_made"), 1)
                eng.wait_ge(c.sem("max_made"), after(c, "max_made"))
            if n >= 1:
                m = n - 1
                w = self.geometry(self.its[m][1])[2]
                i = m % 2
                eng.wait_ge(c.sem("sink_exp"), m + 1)
                eng.tensor_tensor(self.ri[:, i:i + 1], self.sum[:, i:i + 1], self.es[:, i:i + 1], ALU.add) \
                   .then_inc(c.sem("dve_step"), 1)
                eng.wait_ge(c.sem("dve_step"), after(c, "dve_step"))
                eng.reciprocal(self.ri[:, i:i + 1], self.ri[:, i:i + 1]).then_inc(c.sem("dve_step"), 1)
                eng.wait_ge(c.sem("dve_step"), after(c, "dve_step"))
                p = self.p[i][:, 0:2 * w]
                eng.tensor_scalar(p, p, self.ri[:, i:i + 1], None, ALU.mult).then_inc(c.sem("p_made"), 1)
                eng.wait_ge(c.sem("p_made"), after(c, "p_made"))
            if n % 8 == 4 and n >= 8:
                pair_out(n // 8 - 1)
        pair_out(7)


class MlstmIn(Stage):

    def __init__(self, c):
        self.c = c
        w = c.dram["w_in_2"].rearrange("(k p) n -> p k n", p=P)
        for i, (name, col) in enumerate((("mq", C2_MQ), ("mk", C2_MK), ("mv0", C2_MV), ("mv1", C2_MV + 512))):
            c.plan(name, w[:, :, col:col + 512], KT, 512, ("ml_made", (4, 10, 16, 22)[i]), slots=4)
        self.h, self.hc = c.at(B_H, KT, SEQ), c.at(B_HC, KT, CTX)
        self.vm = c.at(B_VM, 6, MH, DV + 1)
        self.ktok = c.at(B_KTOK, 6, MH * QK)
        self.qmt = c.at(B_QMT, MH, SEQ)
        self.kmt = c.ext(0, MH, SEQ)
        self.wg = c.ext(6144, KT, 16)
        self.bias = c.ext(6272, 16)
        self.g = c.small[:, 42:138].rearrange("p (t n) -> p t n", t=6)
        self.lf = c.small[:, 138:186].rearrange("p (t w n) -> p t w n", t=6, w=2)
        self.tmp = c.ext(6288, 6, 2, 4)
        self.tm2 = c.ext(6336, 6, 2, 4)

    def pool(self, eng):
        c, d = self.c, self.c.dram
        eng.dma_start(self.wg, d["w_in_2"].rearrange("(k p) n -> p k n", p=P)[:, :, C2_MG:C2_MG + 16]) \
           .then_inc(c.sem("mg_loaded"), 16)
        b = d["ml_gate_b_2"].rearrange("a b n -> (a b n)").rearrange("(a n) -> a n", a=1)
        eng.dma_start(self.bias, b.to_broadcast([P, 16])).then_inc(c.sem("mg_loaded"), 16)
        eng.memset(self.vm[:, :, :, DV:DV + 1], 1.0).then_inc(c.sem("pool_step"), 1)
        eng.wait_ge(c.sem("pool_step"), after(c, "pool_step"))

    def pe(self, eng):
        c = self.c
        n = 0
        for h in range(MH):
            w = c.weights(eng, "mq")
            if n >= 2:
                eng.wait_ge(c.sem("ml_taken"), n - 1)
            feature_tile(eng, c.psum[:, n % 2, :], w, h * P, self.h).then_inc(c.sem("ml_made"), 1)
            n += 1
        for name in ("mk", "mv0", "mv1"):
            w = c.weights(eng, name)
            for t in range(6):
                eng.wait_ge(c.sem("ml_taken"), n - 1)
                lhs = self.h if t < TT else self.hc
                token_tile(eng, c.psum[:, n % 2, :], lhs, t % TT, w).then_inc(c.sem("ml_made"), 1)
                n += 1
            if name == "mk":
                self.gates_and_keys(eng)

    def gates_and_keys(self, eng):
        c = self.c
        eng.wait_ge(c.sem("mg_loaded"), 32)
        for t in range(6):
            lhs = self.h if t < TT else self.hc
            ins = token_tile(eng, c.psum[:, 4, t * 16:(t + 1) * 16], lhs, t % TT, self.wg)
        ins.then_inc(c.sem("mg_made"), 1)
        eng.wait_ge(c.sem("ml_taken"), 10)
        for h in range(MH):
            if h >= 2:
                eng.wait_ge(c.sem("kmt_taken"), h - 1)
            for t in range(TT):
                ins = eng.transpose(c.psum[:, 2 + h % 2, t * P:(t + 1) * P], self.ktok[:, t, h * QK:(h + 1) * QK],
                                    c.ident)
            ins.then_inc(c.sem("kmt_turned"), 1)

    def act(self, eng):
        c = self.c
        for n in range(22):
            eng.wait_ge(c.sem("ml_made"), n + 1)
            src = c.psum[:, n % 2, :]
            if n < 4:
                ins = eng.activation(self.qmt[:, n, :], src, ACT.Copy)
            elif n < 10:
                ins = eng.activation(self.ktok[:, n - 4, :], src, ACT.Copy, scale=QK ** -0.5)
            else:
                half, t = (n - 10) // 6, (n - 10) % 6
                ins = eng.activation(self.vm[:, t, 2 * half:2 * half + 2, 0:DV],
                                     src.rearrange("p (h d) -> p h d", h=2), ACT.Copy)
            ins.then_inc(c.sem("ml_taken"), 1)
            eng.wait_ge(c.sem("ml_taken"), after(c, "ml_taken"))
            if n == 9:
                self.take_keys(eng)

    def take_keys(self, eng):
        c = self.c
        for h in range(MH):
            eng.wait_ge(c.sem("kmt_turned"), h + 1)
            eng.activation(self.kmt[:, h, :], c.psum[:, 2 + h % 2, :], ACT.Copy).then_inc(c.sem("kmt_taken"), 1)
            eng.wait_ge(c.sem("kmt_taken"), after(c, "kmt_taken"))
        eng.wait_ge(c.sem("f_split"), 1)
        eng.activation(self.tmp, self.tmp, ACT.Exp).then_inc(c.sem("act_step"), 1)
        eng.wait_ge(c.sem("act_step"), after(c, "act_step"))
        eng.activation(self.tmp, self.tmp, ACT.Ln, bias=c.one).then_inc(c.sem("f_log"), 1)
        eng.wait_ge(c.sem("f_log"), after(c, "f_log"))

    def dve(self, eng):
        c = self.c
        eng.wait_ge(c.sem("mg_made"), 1)
        eng.tensor_tensor(self.g, c.psum[:, 4, 0:96].rearrange("p (t n) -> p t n", t=6),
                          self.bias.unsqueeze(1).to_broadcast([P, 6, 16]), ALU.add).then_inc(c.sem("dve_step"), 1)
        eng.wait_ge(c.sem("dve_step"), after(c, "dve_step"))
        f = self.g.rearrange("p t (w i n) -> p t w i n", w=2, i=2)[:, :, :, 1, :]
        eng.tensor_scalar(self.lf, f, 0.0, None, ALU.min).then_inc(c.sem("dve_step"), 1)
        eng.wait_ge(c.sem("dve_step"), after(c, "dve_step"))
        eng.tensor_scalar(self.tm2, f, 0.0, None, ALU.max).then_inc(c.sem("dve_step"), 1)
        eng.wait_ge(c.sem("dve_step"), after(c, "dve_step"))
        eng.tensor_tensor(self.tmp, self.lf, self.tm2, ALU.subtract).then_inc(c.sem("f_split"), 1)
        eng.wait_ge(c.sem("f_split"), after(c, "f_split"))
        eng.wait_ge(c.sem("f_log"), 1)
        eng.tensor_tensor(self.lf, self.lf, self.tmp, ALU.subtract).then_inc(c.sem("dve_step"), 1)
        eng.wait_ge(c.sem("dve_step"), after(c, "dve_step"))


class MlstmScan(Stage):

    def __init__(self, c):
        self.c = c
        self.vm = c.at(B_VM, 6, MH, DV + 1)
        self.ktok = c.at(B_KTOK, 6, MH, QK)
        self.qmt = c.at(B_QMT, MH, SEQ)
        self.kmt = c.ext(0, MH, SEQ)
        self.h = c.ext(2048, TT, D)
        self.g = c.small[:, 42:138].rearrange("p (t w i n) -> p t w i n", t=6, w=2, i=2)
        self.lf = c.small[:, 138:186].rearrange("p (t w n) -> p t w n", t=6, w=2)
        self.state = c.at(B_HC, MH, DV + 1)
        self.dg = c.ext(6144, MH, P)
        self.dm = c.ext(6656, MH, P)
        self.st = c.ext(7168, MH, P)
        self.stt = c.ext(7680, MH, P)
        self.hn = c.at(B_T, MH, DV + 1)
        b = B_HC + MH * (DV + 1)
        self.kw = c.at(b, MH, QK)
        b += MH * QK
        self.q = {}
        for n in ("b", "e", "m", "mx", "mq", "mm", "den", "neg"):
            self.q[n] = c.at(b, MH)
            b += MH
        self.bb = c.at(b, 12, 2, MH)
        b += 12 * 2 * MH
        self.arg = c.at(b, 4, MH)
        self.w = [c.at(b + 16 + 16 * i, 4, MH) for i in range(2)]
        self.steps = [(0, t) for t in (4, 5, 0, 1, 2, 3)] + [(1, t) for t in (5, 4, 3, 2, 1, 0)]
        self.lat = [t < TT for _, t in self.steps]
        w = c.dram["w_in_2"].rearrange("(k p) n -> p k n", p=P)
        for i in range(2):
            c.plan(("mo", i), w[:, :, C2_MO + 512 * i:C2_MO + 512 * (i + 1)], KT, 512, ("mo_made", 4 * (i + 1)),
                   slots=4)
        c.gate_slot = c.loads["mv0"]["slot"]
        self.o = c.slot(c.gate_slot, KT, SEQ)
        self.x = c.at(B_H, KT, SEQ)

    def outs_before(self, n):
        return sum(self.lat[:n])

    def pe(self, eng):
        c = self.c
        for n, (way, t) in enumerate(self.steps):
            at = 2 * MH * n
            eng.matmul(c.psum[:, 3, at:at + MH], c.since if way else c.upto, self.lf[:, t, way, :], start=True,
                       stop=True)
            ins = eng.matmul(c.psum[:, 3, at + MH:at + 2 * MH], c.ones, self.lf[:, t, way, :], start=True, stop=True)
        ins.then_inc(c.sem("ms_sums_made"), 1)
        self.pe_first(eng, 0)
        self.pe_second(eng, 0)
        self.pe_third(eng, 0)
        for n in range(len(self.steps)):
            more = n + 1 < len(self.steps)
            if more:
                self.pe_first(eng, n + 1)
            if self.lat[n]:
                self.pe_outputs(eng, n)
            if more:
                self.pe_second(eng, n + 1)
            self.pe_update(eng, n)
            if self.lat[n]:
                self.gate_tile(eng, self.outs_before(n))
            if more:
                self.pe_third(eng, n + 1)

    def gate_tile(self, eng, f):
        c = self.c
        w = c.weights(eng, ("mo", f // 4))
        if f >= 1:
            eng.wait_ge(c.sem("ms_o_taken"), f)
        feature_tile(eng, c.psum[:, 0, :], w, f % 4 * P, self.x).then_inc(c.sem("mo_made"), 1)

    def pe_first(self, eng, n):
        c = self.c
        t = self.steps[n][1]
        tok = slice(t * P, (t + 1) * P)
        if self.lat[n]:
            if self.outs_before(n) >= 1:
                eng.wait_ge(c.sem("ms_s_made"), self.outs_before(n))
            for h in range(MH):
                ins = eng.matmul(c.psum[:, 2, h * P:(h + 1) * P], self.qmt[:, h, tok], self.kmt[:, h, tok],
                                 start=True, stop=True)
            ins.then_inc(c.sem("ms_qk_made"), 1)

    def pe_second(self, eng, n):
        c = self.c
        eng.wait_ge(c.sem("ms_diag_made"), n + 1)
        eng.matmul(c.psum[:, 1, :], c.ones, self.dg.rearrange("p h n -> p (h n)"), start=True,
                   stop=True).then_inc(c.sem("ms_row_made"), 1)

    def pe_third(self, eng, n):
        c = self.c
        if self.lat[n]:
            done = self.outs_before(n)
            eng.wait_ge(c.sem("ms_s_made"), done + 1)
            if done >= 1:
                eng.wait_ge(c.sem("ms_st_taken"), done)
            for h in range(MH):
                ins = eng.transpose(c.psum[:, 3, h * P:(h + 1) * P], self.st[:, h, :], c.ident)
            ins.then_inc(c.sem("ms_s_turned"), 1)

    def pe_outputs(self, eng, n):
        c = self.c
        t = self.steps[n][1]
        outs = self.outs_before(n)
        eng.wait_ge(c.sem("ms_st_taken"), outs + 1)
        if n >= 1:
            eng.wait_ge(c.sem("ms_state_done"), MH * n)
        for h in range(MH):
            done = MH * outs + h
            if done >= 2:
                eng.wait_ge(c.sem("ms_h_taken"), done - 1)
            eng.matmul(c.psum[:, 4 + h % 2, 0:DV + 1], self.stt[:, h, :], self.vm[:, t, h, :], start=True,
                       stop=True)
            eng.matmul(c.psum[:, 6 + h % 2, 0:DV + 1], self.qmt[:, h, t * P:(t + 1) * P], self.state[:, h, :],
                       start=True, stop=True).then_inc(c.sem("ms_h_made"), 1)

    def pe_update(self, eng, n):
        c = self.c
        t = self.steps[n][1]
        eng.wait_ge(c.sem("ms_kw_made"), n + 1)
        for h in range(MH):
            if h < 2 and self.outs_before(n + 1):
                eng.wait_ge(c.sem("ms_h_taken"), MH * self.outs_before(n + 1) - 1 + h)
            if MH * n + h >= 2:
                eng.wait_ge(c.sem("ms_state_done"), MH * n + h - 1)
            eng.matmul(c.psum[:, 6 + h % 2, 0:DV + 1], self.kw[:, h, :], self.vm[:, t, h, :], start=True,
                       stop=True).then_inc(c.sem("ms_state_made"), 1)

    def act(self, eng):
        c = self.c
        self.act_prepare(eng, 0)
        for n in range(len(self.steps)):
            if self.lat[n]:
                self.act_outputs(eng, n)
            if n + 1 < len(self.steps):
                self.act_prepare(eng, n + 1)
            if self.lat[n]:
                f = self.outs_before(n)
                eng.wait_ge(c.sem("mo_made"), f + 1)
                eng.activation(self.o[:, f, :], c.psum[:, 0, :], ACT.Copy).then_inc(c.sem("ms_o_taken"), 1)
                eng.wait_ge(c.sem("ms_o_taken"), after(c, "ms_o_taken"))

    def act_prepare(self, eng, n):
        c = self.c
        eng.wait_ge(c.sem("ms_args_made"), n + 1)
        eng.activation(self.w[n % 2], self.arg, ACT.Exp).then_inc(c.sem("ms_args_exp"), 1)
        eng.wait_ge(c.sem("ms_args_exp"), after(c, "ms_args_exp"))
        if self.lat[n]:
            eng.activation(self.dm, self.dm, ACT.Exp).then_inc(c.sem("ms_dm_exp"), 1)
            eng.wait_ge(c.sem("ms_dm_exp"), after(c, "ms_dm_exp"))
            eng.wait_ge(c.sem("ms_s_turned"), self.outs_before(n) + 1)
            eng.activation(self.stt.rearrange("p h n -> p (h n)"), c.psum[:, 3, :], ACT.Copy) \
               .then_inc(c.sem("ms_st_taken"), 1)
            eng.wait_ge(c.sem("ms_st_taken"), after(c, "ms_st_taken"))

    def act_outputs(self, eng, n):
        c = self.c
        for h in range(MH):
            done = MH * self.outs_before(n) + h
            eng.wait_ge(c.sem("ms_h_made"), done + 1)
            if h == 0 and done:
                eng.wait_ge(c.sem("ms_h_written"), done // MH)
            eng.activation(self.hn[:, h, :], c.psum[:, 4 + h % 2, 0:DV + 1], ACT.Copy).then_inc(c.sem("ms_h_copied"), 1)
            eng.wait_ge(c.sem("ms_h_copied"), after(c, "ms_h_copied"))

    def pool(self, eng):
        self.pool_prepare(eng, 0)
        for n in range(len(self.steps)):
            if n + 1 < len(self.steps):
                self.pool_diagonals(eng, n + 1)
            if self.lat[n]:
                self.pool_outputs(eng, n)
            if n + 1 < len(self.steps):
                self.pool_keys(eng, n + 1)

    def pool_prepare(self, eng, n):
        self.pool_diagonals(eng, n)
        self.pool_keys(eng, n)

    def pool_diagonals(self, eng, n):
        c = self.c
        eng.wait_ge(c.sem("ms_e_made"), n + 1)
        if n >= 1:
            eng.wait_ge(c.sem("ms_row_made"), n)
        eng.tensor_tensor(self.dg, c.ident.unsqueeze(1).to_broadcast([P, MH, P]), self.wide(self.q["e"]),
                          ALU.mult).then_inc(c.sem("ms_diag_made"), 1)
        eng.wait_ge(c.sem("ms_diag_made"), after(c, "ms_diag_made"))

    def pool_keys(self, eng, n):
        c = self.c
        eng.wait_ge(c.sem("ms_args_exp"), n + 1)
        if n >= 1:
            eng.wait_ge(c.sem("ms_state_made"), MH * n)
        eng.tensor_tensor(self.kw, self.ktok[:, self.steps[n][1], :, :], self.wide(self.w[n % 2][:, 2, :]),
                          ALU.mult).then_inc(c.sem("ms_kw_made"), 1)
        eng.wait_ge(c.sem("ms_kw_made"), after(c, "ms_kw_made"))

    def pool_outputs(self, eng, n):
        c = self.c
        way, t = self.steps[n]
        eng.wait_ge(c.sem("ms_den_made"), self.outs_before(n) + 1)
        dst = self.h[:, t, :].rearrange("p (h d) -> p h d", h=MH)
        part = self.hn[:, :, 0:DV]
        den = self.q["den"].unsqueeze(2).to_broadcast([P, MH, DV])
        if way == 0:
            eng.tensor_tensor(dst, part, den, ALU.mult).then_inc(c.sem("ms_h_written"), 1)
        else:
            eng.tensor_tensor(part, part, den, ALU.mult).then_inc(c.sem("pool_step"), 1)
            eng.wait_ge(c.sem("pool_step"), after(c, "pool_step"))
            eng.tensor_tensor(dst, dst, part, ALU.add).then_inc(c.sem("ms_h_written"), 1)
        eng.wait_ge(c.sem("ms_h_written"), after(c, "ms_h_written"))

    def dve(self, eng):
        c = self.c
        eng.wait_ge(c.sem("ms_sums_made"), 1)
        eng.tensor_copy(self.bb.rearrange("p n w h -> p (n w h)"), c.psum[:, 3, 0:2 * MH * len(self.steps)]) \
           .then_inc(c.sem("dve_step"), 1)
        eng.wait_ge(c.sem("dve_step"), after(c, "dve_step"))
        self.dve_first(eng, 0)
        self.dve_second(eng, 0)
        self.dve_third(eng, 0)
        for n in range(len(self.steps)):
            more = n + 1 < len(self.steps)
            if more:
                self.dve_first(eng, n + 1)
            if self.lat[n]:
                self.dve_outputs(eng, n)
            self.dve_update(eng, n)
            if more:
                self.dve_second(eng, n + 1)
                self.dve_third(eng, n + 1)

    def wide(self, a):
        return a.unsqueeze(2).to_broadcast([P, MH, P])

    def bank(self, b):
        return self.c.psum[:, b, :].rearrange("p (h n) -> p h n", h=MH)

    def dve_first(self, eng, n):
        c, q = self.c, self.q
        way, t = self.steps[n]
        eng.tensor_tensor(q["e"], self.g[:, t, way, 0, :], self.bb[:, n, 0, :], ALU.subtract) \
           .then_inc(c.sem("ms_e_made"), 1)
        eng.wait_ge(c.sem("ms_e_made"), after(c, "ms_e_made"))

    def dve_second(self, eng, n):
        c, q = self.c, self.q
        way, t = self.steps[n]
        b, last = self.bb[:, n, 0, :], self.bb[:, n, 1, :]
        if n % 6 == 0:
            eng.memset(q["m"], 0.0).then_inc(c.sem("dve_step"), 1)
            eng.wait_ge(c.sem("dve_step"), after(c, "dve_step"))
        eng.wait_ge(c.sem("ms_row_made"), n + 1)
        eng.tensor_reduce(q["mx"], self.bank(1), AX.X, ALU.max).then_inc(c.sem("dve_step"), 1)
        eng.wait_ge(c.sem("dve_step"), after(c, "dve_step"))
        eng.tensor_tensor(q["mx"], q["mx"], q["m"], ALU.max).then_inc(c.sem("dve_step"), 1)
        eng.wait_ge(c.sem("dve_step"), after(c, "dve_step"))
        if self.lat[n]:
            mask = (c.mask_ge if way else c.mask_le).unsqueeze(1).to_broadcast([P, MH, P])
            eng.tensor_tensor(self.dm, self.bank(1), mask, ALU.add).then_inc(c.sem("dve_step"), 1)
            eng.wait_ge(c.sem("dve_step"), after(c, "dve_step"))
            eng.tensor_reduce(q["mm"], self.dm, AX.X, ALU.max).then_inc(c.sem("dve_step"), 1)
            eng.wait_ge(c.sem("dve_step"), after(c, "dve_step"))
            eng.tensor_tensor(q["mm"], q["mm"], q["m"], ALU.max).then_inc(c.sem("dve_step"), 1)
            eng.wait_ge(c.sem("dve_step"), after(c, "dve_step"))
            eng.tensor_tensor(self.dm, self.dm, self.wide(q["mm"]), ALU.subtract).then_inc(c.sem("dve_step"), 1)
            eng.wait_ge(c.sem("dve_step"), after(c, "dve_step"))
            eng.tensor_tensor(self.arg[:, 0, :], q["m"], q["mm"], ALU.subtract).then_inc(c.sem("dve_step"), 1)
            eng.wait_ge(c.sem("dve_step"), after(c, "dve_step"))
            eng.scalar_tensor_tensor(self.arg[:, 1, :], b, -1.0, q["mm"], ALU.mult, ALU.subtract) \
               .then_inc(c.sem("dve_step"), 1)
            eng.wait_ge(c.sem("dve_step"), after(c, "dve_step"))
        elif n % 6 == 0:
            eng.memset(self.arg[:, 0:2, :], 0.0).then_inc(c.sem("dve_step"), 1)
            eng.wait_ge(c.sem("dve_step"), after(c, "dve_step"))
        eng.tensor_tensor(self.arg[:, 2, :], q["e"], q["mx"], ALU.subtract).then_inc(c.sem("dve_step"), 1)
        eng.wait_ge(c.sem("dve_step"), after(c, "dve_step"))
        eng.tensor_tensor(self.arg[:, 3, :], q["m"], q["mx"], ALU.subtract).then_inc(c.sem("ms_args_made"), 1)
        eng.wait_ge(c.sem("ms_args_made"), after(c, "ms_args_made"))
        eng.tensor_tensor(q["m"], last, q["mx"], ALU.add).then_inc(c.sem("dve_step"), 1)
        eng.wait_ge(c.sem("dve_step"), after(c, "dve_step"))

    def dve_third(self, eng, n):
        c = self.c
        eng.wait_ge(c.sem("ms_args_exp"), n + 1)
        if self.lat[n]:
            done = self.outs_before(n)
            eng.wait_ge(c.sem("ms_dm_exp"), done + 1)
            eng.wait_ge(c.sem("ms_qk_made"), done + 1)
            if done >= 1:
                eng.wait_ge(c.sem("ms_s_turned"), done)
            eng.tensor_tensor(self.st, self.dm, self.bank(2), ALU.mult).then_inc(c.sem("ms_s_made"), 1)
            eng.wait_ge(c.sem("ms_s_made"), after(c, "ms_s_made"))

    def dve_outputs(self, eng, n):
        c, q = self.c, self.q
        way, t = self.steps[n]
        w = self.w[n % 2]
        for h in range(MH):
            eng.wait_ge(c.sem("ms_h_copied"), MH * self.outs_before(n) + h + 1)
            eng.scalar_tensor_tensor(self.hn[:, h, :], c.psum[:, 6 + h % 2, 0:DV + 1], w[:, 0, h:h + 1],
                                     self.hn[:, h, :], ALU.mult, ALU.add).then_inc(c.sem("ms_h_taken"), 1)
            eng.wait_ge(c.sem("ms_h_taken"), after(c, "ms_h_taken"))
        den, nq = q["den"].unsqueeze(2), self.hn[:, :, DV:DV + 1]
        eng.scalar_tensor_tensor(den, nq, -1.0, nq, ALU.mult, ALU.max).then_inc(c.sem("dve_step"), 1)
        eng.wait_ge(c.sem("dve_step"), after(c, "dve_step"))
        eng.tensor_tensor(q["den"], q["den"], w[:, 1, :], ALU.max).then_inc(c.sem("dve_step"), 1)
        eng.wait_ge(c.sem("dve_step"), after(c, "dve_step"))
        eng.reciprocal(q["den"], q["den"]).then_inc(c.sem("ms_den_made"), 1)
        eng.wait_ge(c.sem("ms_den_made"), after(c, "ms_den_made"))

    def dve_update(self, eng, n):
        c = self.c
        if n % 6 == 0:
            eng.memset(self.state, 0.0).then_inc(c.sem("dve_step"), 1)
            eng.wait_ge(c.sem("dve_step"), after(c, "dve_step"))
        for h in range(MH):
            eng.wait_ge(c.sem("ms_state_made"), MH * n + h + 1)
            eng.scalar_tensor_tensor(self.state[:, h, :], self.state[:, h, :], self.w[n % 2][:, 3, h:h + 1],
                                     c.psum[:, 6 + h % 2, 0:DV + 1], ALU.mult, ALU.add) \
               .then_inc(c.sem("ms_state_done"), 1)
            eng.wait_ge(c.sem("ms_state_done"), after(c, "ms_state_done"))


class MlstmOut(Stage):

    def __init__(self, c):
        self.c = c
        self.h = c.ext(2048, TT, D)
        self.ml = c.at(B_ML, KT, SEQ)
        self.o = c.slot(c.gate_slot, KT, SEQ)
        self.sq = c.at(B_Y + 4096, DV)

    def pe(self, eng):
        c = self.c
        for f in range(KT):
            if f == 0:
                eng.wait_ge(c.sem("mh_scaled"), TT)
            if f >= 2:
                eng.wait_ge(c.sem("ml_out"), f - 1)
            for t in range(TT):
                ins = eng.transpose(c.psum[:, 2 + f % 2, t * P:(t + 1) * P], self.h[:, t, f * P:(f + 1) * P], c.ident)
            ins.then_inc(c.sem("mh_turned"), 1)

    def act(self, eng):
        c = self.c
        for n in range(TT * MH):
            t, h = n // MH, n % MH
            eng.activation(self.sq, self.h[:, t, h * DV:(h + 1) * DV], ACT.Square,
                           accum_out=c.ss[:, n:n + 1]).then_inc(c.sem("act_step"), 1)
            eng.wait_ge(c.sem("act_step"), after(c, "act_step"))
        eng.activation(c.rs[:, 0:16], c.ss[:, 0:16], ACT.Sqrt, scale=1.0 / DV, bias=c.eps).then_inc(c.sem("mh_rs"), 1)
        eng.wait_ge(c.sem("mh_rs"), after(c, "mh_rs"))
        for f in range(KT):
            eng.activation(self.o[:, f, :], self.o[:, f, :], ACT.Sigmoid).then_inc(c.sem("mo_sig"), 1)

    def dve(self, eng):
        c = self.c
        eng.wait_ge(c.sem("mh_rs"), 1)
        invert(c, eng, c.rs[:, 0:16])
        for t in range(TT):
            v = self.h[:, t, :].rearrange("p (h d) -> p h d", h=MH)
            eng.tensor_tensor(v, v, c.rs[:, MH * t:MH * (t + 1)].unsqueeze(2).to_broadcast([P, MH, DV]),
                              ALU.mult).then_inc(c.sem("mh_scaled"), 1)
            eng.wait_ge(c.sem("mh_scaled"), after(c, "mh_scaled"))
        for f in range(KT):
            eng.wait_ge(c.sem("mh_turned"), f + 1)
            eng.wait_ge(c.sem("mo_sig"), f + 1)
            eng.scalar_tensor_tensor(self.ml[:, f, :], c.psum[:, 2 + f % 2, :], c.v("ml_norm_w_2", f),
                                     self.o[:, f, :], ALU.mult, ALU.mult).then_inc(c.sem("ml_out"), 1)
            eng.wait_ge(c.sem("ml_out"), after(c, "ml_out"))


class Merge(Stage):

    def __init__(self, c):
        self.c = c
        w = c.dram["w_in_2"].rearrange("(k p) n -> p k n", p=P)
        fold = lambda name: c.dram[name].rearrange("(k p) n -> p k n", p=P)
        self.parts = [("ga", w, C2_GA), ("gm", w, C2_GM), ("ba", fold("w_branch_att_2"), 0),
                      ("bm", fold("w_branch_ml_2"), 0)]
        last = c.order.index("MlstmOut")
        c.turn = (c.gate_slot + 1) % 4
        busy = {c.gate_slot, 4, 5}
        for i in range(2):
            for n, (name, src, col) in enumerate(self.parts):
                c.plan((name, i), src[:, :, col + 512 * i:col + 512 * (i + 1)], KT, 512,
                       ("merge_made", 4 * (4 * i + 3) + n + 1), slots=SLOTS,
                       stage=last if c.turn % SLOTS in busy else None)
                busy.discard(c.loads[(name, i)]["slot"])
        for i in range(2):
            c.plan(("wo2", i), fold("w_out_2")[:, :, 512 * i:512 * (i + 1)], KT, 512, ("wo2_made", 4 * (i + 1)))
        self.x, self.h = c.at(B_X, KT, SEQ), c.at(B_H, KT, SEQ)
        self.att, self.ml, self.y = c.at(B_ATT, KT, SEQ), c.at(B_ML, KT, SEQ), c.at(B_Y, KT, SEQ)
        self.sg = [c.at(B_Y + 4096 + 512 * i, 512) for i in range(4)]
        self.u = [c.at(B_HC + 512 * i, 512) for i in range(2)]

    def pe(self, eng):
        c = self.c
        for f in range(KT):
            if f >= 2:
                eng.wait_ge(c.sem("merge_taken"), f - 1)
            for n, (name, _, _) in enumerate(self.parts):
                w = c.weights(eng, (name, f // 4))
                rhs = (self.h, self.h, self.att, self.ml)[n]
                feature_tile(eng, c.psum[:, 4 * (f % 2) + n, :], w, f % 4 * P, rhs).then_inc(c.sem("merge_made"), 1)
        eng.wait_ge(c.sem("merge_taken"), KT)
        for f in range(KT):
            w = c.weights(eng, ("wo2", f // 4))
            if f >= 2:
                eng.wait_ge(c.sem("wo2_taken"), f - 1)
            feature_tile(eng, c.psum[:, f % 2, :], w, f % 4 * P, self.y).then_inc(c.sem("wo2_made"), 1)

    def act(self, eng):
        c = self.c
        for f in range(KT):
            for n in range(2):
                eng.wait_ge(c.sem("merge_made"), 4 * f + n + 1)
                if f >= 2:
                    eng.wait_ge(c.sem("merge_taken"), f - 1)
                eng.activation(self.sg[2 * (f % 2) + n], c.psum[:, 4 * (f % 2) + n, :], ACT.Sigmoid) \
                   .then_inc(c.sem("merge_sig"), 1)
                eng.wait_ge(c.sem("merge_sig"), after(c, "merge_sig"))

    def dve(self, eng):
        c = self.c
        for f in range(KT):
            for n in range(2):
                eng.wait_ge(c.sem("merge_made"), 4 * f + 2 + n + 1)
                eng.wait_ge(c.sem("merge_sig"), 2 * f + n + 1)
                eng.tensor_tensor(self.u[n], self.sg[2 * (f % 2) + n], c.psum[:, 4 * (f % 2) + 2 + n, :],
                                  ALU.mult).then_inc(c.sem("dve_step"), 1)
                eng.wait_ge(c.sem("dve_step"), after(c, "dve_step"))
            eng.tensor_tensor(self.y[:, f, :], self.u[0], self.u[1], ALU.add).then_inc(c.sem("merge_taken"), 1)
            eng.wait_ge(c.sem("merge_taken"), after(c, "merge_taken"))
        for f in range(KT):
            eng.wait_ge(c.sem("wo2_made"), f + 1)
            eng.scalar_tensor_tensor(self.x[:, f, :], c.psum[:, f % 2, :], c.mod[:, MOD["g1"] + f, 0:1],
                                     self.x[:, f, :], ALU.mult, ALU.add).then_inc(c.sem("wo2_taken"), 1)
            eng.wait_ge(c.sem("wo2_taken"), after(c, "wo2_taken"))


class FfnUp(Stage):

    def __init__(self, c):
        self.c = c
        w = c.dram["w_up_2"].rearrange("(k p) n -> p k n", p=P)
        for i in range(6):
            n = min(4, FT - 4 * i)
            for j, part in enumerate("ag"):
                lo = j * DFF + 512 * i
                c.plan((part, i), w[:, :, lo:lo + n * P], KT, n * P, ("up_made_" + part, 4 * i + n))
        self.h = c.at(B_H, KT, SEQ)
        self.act_t = c.at(B_ACT, FT, SEQ)
        self.acc = {p: [c.at(B_FT + 1024 * j + 512 * i, 512) for i in range(2)] for j, p in enumerate("ag")}
        self.sg = [c.at(B_FT + 2048 + 512 * i, 512) for i in range(2)]

    def pe(self, eng):
        c = self.c
        for f in range(FT):
            for j, part in enumerate("ag"):
                w = c.weights(eng, (part, f // 4))
                if f >= 2:
                    eng.wait_ge(c.sem("up_taken_" + part), f - 1)
                feature_tile(eng, c.psum[:, 2 * j + f % 2, :], w, f % 4 * P, self.h) \
                   .then_inc(c.sem("up_made_" + part), 1)

    def act(self, eng):
        c = self.c
        for f in range(FT):
            eng.wait_ge(c.sem("up_taken_g"), f + 1)
            if f >= 2:
                eng.wait_ge(c.sem("ffn_act"), f - 1)
            eng.activation(self.sg[f % 2], self.acc["g"][f % 2], ACT.Silu).then_inc(c.sem("up_silu"), 1)

    def dve(self, eng):
        c = self.c

        def join(f):
            eng.wait_ge(c.sem("up_silu"), f + 1)
            eng.tensor_tensor(self.act_t[:, f, :], self.sg[f % 2], self.acc["a"][f % 2], ALU.mult) \
               .then_inc(c.sem("ffn_act"), 1)
            eng.wait_ge(c.sem("ffn_act"), after(c, "ffn_act"))

        for f in range(FT):
            for j, part in enumerate("ag"):
                tile = j * FT + f
                p, a = c.psum[:, 2 * j + f % 2, :], self.acc[part][f % 2]
                eng.wait_ge(c.sem("up_made_" + part), f + 1)
                eng.tensor_scalar(a, p, c.v("conv_w_2a", 44 + tile), c.v("conv_b_2", tile), ALU.mult,
                                  ALU.add).then_inc(c.sem("dve_step"), 1)
                eng.wait_ge(c.sem("dve_step"), after(c, "dve_step"))
                eng.scalar_tensor_tensor(a[:, 1:], p[:, :SEQ - 1], c.v("conv_w_2a", tile), a[:, 1:],
                                         ALU.mult, ALU.add).then_inc(c.sem("dve_step"), 1)
                eng.wait_ge(c.sem("dve_step"), after(c, "dve_step"))
                eng.scalar_tensor_tensor(a[:, :SEQ - 1], p[:, 1:], c.v("conv_w_2b", tile), a[:, :SEQ - 1],
                                         ALU.mult, ALU.add).then_inc(c.sem("up_taken_" + part), 1)
                eng.wait_ge(c.sem("up_taken_" + part), after(c, "up_taken_" + part))
            if f >= 1:
                join(f - 1)
        join(FT - 1)


class FfnDown(Stage):

    def __init__(self, c):
        self.c = c
        w = c.dram["w_down_2"].rearrange("(k p) n -> p k n", p=P)
        for i in range(6):
            n = min(4, FT - 4 * i)
            c.plan(("fd", i), w[:, 4 * i:4 * i + n, :], n, D, ("fd_step", 4 * i + n))
        self.x, self.act_t = c.at(B_X, KT, SEQ), c.at(B_ACT, FT, SEQ)

    def pe(self, eng):
        c = self.c
        for k in range(FT):
            w = c.weights(eng, ("fd", k // 4))
            for f in range(KT):
                ins = eng.matmul(c.psum[:, f, :], w[:, k % 4, f * P:(f + 1) * P], self.act_t[:, k, :], start=k == 0,
                                 stop=k == FT - 1)
            ins.then_inc(c.sem("fd_step"), 1)

    def dve(self, eng):
        c = self.c
        eng.wait_ge(c.sem("fd_step"), FT)
        for f in range(KT):
            eng.scalar_tensor_tensor(self.x[:, f, :], c.psum[:, f, :], c.mod[:, MOD["g2"] + f, 0:1],
                                     self.x[:, f, :], ALU.mult, ALU.add).then_inc(c.sem("dve_step"), 1)
            eng.wait_ge(c.sem("dve_step"), after(c, "dve_step"))


STAGES = [Normalise1,
          Project1,
          Scan1,
          Out1,
          Route,
          Experts,
          Combine,
          Norm2,
          AttendIn,
          Attend,
          MlstmIn,
          MlstmScan,
          MlstmOut,
          Merge,
          Norm2Ffn,
          FfnUp,
          FfnDown,
          Finish]


def build(nc, dram):
    c = Core(nc, dram)
    c.order = [S.__name__ for S in STAGES]
    stages = []
    for S in STAGES:
        c.building = S.__name__
        stages.append(S(c))

    with nc.Block() as block:
        @block.sync
        def _(sp):
            for stage in stages:
                stage.sync(sp)

        @block.gpsimd
        def _(pool):
            for c.stage, stage in enumerate(stages):
                stage.pool(pool)
                if c.stage >= 1:
                    c.clear(pool, c.stage - 1)
                c.barrier(pool, c.stage + 1)

        @block.scalar
        def _(act):
            for c.stage, stage in enumerate(stages):
                stage.act(act)
                c.barrier(act, c.stage + 1)

        @block.vector
        def _(dve):
            for c.stage, stage in enumerate(stages):
                stage.dve(dve)
                c.barrier(dve, c.stage + 1)

        @block.tensor
        def _(pe):
            for c.stage, stage in enumerate(stages):
                stage.pe(pe)
                c.barrier(pe, c.stage + 1)


def kernel(**inputs):
    import numpy as _np
    import concourse.bacc as _bacc
    from concourse import mybir as _mybir
    from concourse.bass_utils import run_bass_kernel_spmd as _run

    nc = _bacc.Bacc("TRN2", target_bir_lowering=False, num_devices=1)
    arrays, dram = {}, {}
    given = {k: v for k, v in inputs.items()}
    given.update(shape_constants())
    for name, a in given.items():
        a = _np.ascontiguousarray(a)
        if a.ndim > 1 and a.shape[0] == 1:
            a = a.reshape(a.shape[1:])
        arrays[f"in_{name}_dram"] = a
        dram[name] = nc.dram_tensor(f"in_{name}_dram", a.shape, _mybir.dt.from_np(a.dtype), kind="ExternalInput").ap()
    dram["out"] = nc.dram_tensor("out_dram", (SEQ, D), F32, kind="ExternalOutput").ap()
    dram["y_rows"] = nc.dram_tensor("y_rows_dram", (PAIRS + ROWS, D), F32, kind="Internal").ap()
    build(nc, dram)
    r = _run(nc, [arrays], core_ids=[0])
    return r.results[0]["out_dram"].reshape(1, SEQ, D)
```
